# Optimizing a Trainium2 kernel written in Bass

```python
import math
import jax
import jax.numpy as jnp
from jax import lax
import numpy as np

D_MODEL = 1024
BATCH = 1
SEQ = 256
DEPTH = 1
DEC_BATCH = 8
DEC_SEQ = 1
PAST_LEN = 2048
PAGE_SIZE = 128

CONV_CH = 384
CONV_WIDTH = 31
DIL_GROUPS = ((128, 1), (512, 4), (2048, 16))
DIL_HPG = 4
DIL_HEAD_DIM = 32
DIL_HEADS = 12
DIL_WIDTH = 384
MOBA_HEADS = 4
MOBA_HEAD_DIM = 64
MOBA_WIDTH = 256
MOBA_BLOCK = 256
MOBA_TOP_K = 3
MOBA_Q_CHUNK = 32
FF_HIDDEN = 4 * D_MODEL
N_BRANCH = 3
REL_BUCKETS = 32
REL_MAX_EXACT = 16
REL_MAX_DIST = 2048
N_ATT_HEADS = DIL_HEADS + MOBA_HEADS
NORM_EPS = 1e-6
IN_COLS = 2 * CONV_CH + 3 * DIL_WIDTH + 3 * MOBA_WIDTH + N_BRANCH * D_MODEL

kernel_name = 'gated_parallel_conv_dilated_moba_decoder_step'

F32 = jnp.float32

def _rmsnorm(x, g):
    xf = x.astype(F32)
    y = xf * lax.rsqrt(jnp.mean(xf * xf, axis=-1, keepdims=True) + NORM_EPS)
    return (y * g.astype(F32)).astype(x.dtype)

def _layernorm(x, g, b):
    xf = x.astype(F32)
    mu = jnp.mean(xf, axis=-1, keepdims=True)
    xc = xf - mu
    var = jnp.mean(xc * xc, axis=-1, keepdims=True)
    return (xc * lax.rsqrt(var + NORM_EPS) * g.astype(F32) + b.astype(F32)).astype(x.dtype)

def _rel_bucket(dist):
    n = jnp.maximum(dist, 0)
    nf = jnp.maximum(n, 1).astype(F32)
    ratio = math.log(REL_MAX_DIST / REL_MAX_EXACT)
    large = REL_MAX_EXACT + (jnp.log(nf / REL_MAX_EXACT) / ratio * (REL_BUCKETS - REL_MAX_EXACT)).astype(jnp.int32)
    large = jnp.minimum(large, REL_BUCKETS - 1)
    return jnp.where(n < REL_MAX_EXACT, n, large)

def _project(x, norm_g, w_in, b_gate, dqn, dkn, mqn, mkn):
    n, l, _ = x.shape
    h = _rmsnorm(x, norm_g)
    z = h @ w_in
    sizes = (CONV_CH, CONV_CH, DIL_WIDTH, DIL_WIDTH, DIL_WIDTH, MOBA_WIDTH, MOBA_WIDTH, MOBA_WIDTH)
    cuts = [int(c) for c in np.cumsum(sizes)]
    a, b, dq, dk, dv, mq, mk, mv, gl = jnp.split(z, cuts, axis=-1)
    u = a * jax.nn.sigmoid(b)
    dq = _rmsnorm(dq.reshape(n, l, DIL_HEADS, DIL_HEAD_DIM), dqn)
    dk = _rmsnorm(dk.reshape(n, l, DIL_HEADS, DIL_HEAD_DIM), dkn)
    dv = dv.reshape(n, l, DIL_HEADS, DIL_HEAD_DIM)
    mq = _rmsnorm(mq.reshape(n, l, MOBA_HEADS, MOBA_HEAD_DIM), mqn)
    mk = _rmsnorm(mk.reshape(n, l, MOBA_HEADS, MOBA_HEAD_DIM), mkn)
    mv = mv.reshape(n, l, MOBA_HEADS, MOBA_HEAD_DIM)
    gates = jax.nn.sigmoid(gl + b_gate).reshape(n, l, N_BRANCH, D_MODEL)
    return u, dq, dk, dv, mq, mk, mv, gates

def _conv_branch(u_ext, conv_w, conv_b, ln_g, ln_b, w_conv_out):
    c = lax.conv_general_dilated(u_ext, conv_w[:, None, :].astype(u_ext.dtype), (1,), 'VALID',
                                 dimension_numbers=('NWC', 'WIO', 'NWC'),
                                 feature_group_count=CONV_CH) + conv_b
    c = _layernorm(c, ln_g, ln_b)
    return jax.nn.silu(c) @ w_conv_out

def _dilated_group_prompt(q, k, v, dil, span, tab_hT):
    n, s, h, e = q.shape
    lsub = s // dil
    nc = -(-lsub // span)
    lp = nc * span

    def to_sub(a):
        a = a.reshape(n, lsub, dil, h, e).transpose(0, 2, 1, 3, 4)
        a = jnp.pad(a, ((0, 0), (0, 0), (0, lp - lsub), (0, 0), (0, 0)))
        return a.reshape(n, dil, nc, span, h, e)

    def band(a):
        prev = jnp.pad(a, ((0, 0), (0, 0), (1, 0), (0, 0), (0, 0), (0, 0)))[:, :, :nc]
        return jnp.concatenate([prev, a], axis=3)

    qs, ks_, vs = to_sub(q), to_sub(k), to_sub(v)
    kb, vb = band(ks_), band(vs)
    qi = jnp.arange(span)[:, None]
    ki = jnp.arange(2 * span)[None, :]
    rel = qi + span - ki
    in_band = (rel >= 0) & (rel <= span)
    after_start = (jnp.arange(nc)[:, None, None] > 0) | (ki >= span)[None]
    mask = in_band[None] & after_start
    bias = tab_hT[:, _rel_bucket(rel * dil)]
    logits = jnp.einsum('nrcqhe,nrckhe->nrchqk', qs, kb).astype(F32) * (e ** -0.5) + bias
    logits = jnp.where(mask[:, None], logits, -jnp.inf)
    lse = jax.nn.logsumexp(logits, axis=-1)
    p = jnp.exp(logits - lse[..., None]).astype(v.dtype)
    o = jnp.einsum('nrchqk,nrckhe->nrcqhe', p, vb)
    o = o.reshape(n, dil, lp, h, e)[:, :, :lsub].transpose(0, 2, 1, 3, 4).reshape(n, s, h, e)
    lse = lse.transpose(0, 1, 2, 4, 3).reshape(n, dil, lp, h)[:, :, :lsub]
    lse = lse.transpose(0, 2, 1, 3).reshape(n, s, h)
    return o, lse

def _dilated_group_sample(q, ke, ve, wb, dil, span, tab_hT):
    t = q.shape[1]
    e = q.shape[-1]
    j = jnp.arange(span + 1)
    idx = wb + jnp.arange(t)[:, None] - j[None, :] * dil
    ok = idx >= 0
    idx = jnp.maximum(idx, 0)
    kg = ke[:, idx]
    vg = ve[:, idx]
    bias = tab_hT[:, _rel_bucket(j * dil)]
    logits = jnp.einsum('nthe,ntjhe->nthj', q, kg).astype(F32) * (e ** -0.5) + bias
    logits = jnp.where(ok[None, :, None, :], logits, -jnp.inf)
    lse = jax.nn.logsumexp(logits, axis=-1)
    p = jnp.exp(logits - lse[..., None]).astype(ve.dtype)
    o = jnp.einsum('nthj,ntjhe->nthe', p, vg)
    return o, lse

def _combine_dilated(outs, lses, w_dil_out):
    a = jax.nn.softmax(jnp.stack(lses), axis=0)
    o = jnp.einsum('gnlh,gnlhe->nlhe', a, jnp.stack(outs).astype(F32)).astype(outs[0].dtype)
    n, l, h, e = o.shape
    return o.reshape(n, l, h * e) @ w_dil_out

def _moba_route(q, kmean, own, ks):
    nb = kmean.shape[1]
    s = jnp.einsum('nqhe,njhe->nqhj', q.astype(F32), kmean)
    past = jnp.arange(nb)[None, :] < own[:, None]
    s = jnp.where(past[None, :, None, :], s, -jnp.inf)
    _, sel = lax.top_k(s, ks)
    ok = sel < own[None, :, None, None]
    return sel, ok

def _moba_attend(q, q_pos, k_sel, v_sel, sel, ok, k_own, v_own, own, tab_hT):
    n, nq, h, e = q.shape
    ks = sel.shape[-1]
    scale = e ** -0.5
    r = jnp.arange(MOBA_BLOCK)
    d_sel = q_pos[:, None, None, None] - (sel[..., None] * MOBA_BLOCK + r)
    hh = jnp.arange(h)[:, None, None]
    ls = jnp.einsum('nqhe,nqhske->nqhsk', q, k_sel).astype(F32) * scale + tab_hT[hh, _rel_bucket(d_sel)]
    ls = jnp.where(ok[..., None] & (d_sel >= 0), ls, -jnp.inf)
    d_own = q_pos[:, None] - (own[:, None] * MOBA_BLOCK + r)
    shared_own = k_own.shape[1] == 1
    if shared_own:
        lo = jnp.einsum('nqhe,nkhe->nqhk', q, k_own[:, 0])
    else:
        lo = jnp.einsum('nqhe,nqkhe->nqhk', q, k_own)
    lo = lo.astype(F32) * scale + jnp.transpose(tab_hT[:, _rel_bucket(d_own)], (1, 0, 2))
    lo = jnp.where((d_own >= 0)[:, None, :], lo, -jnp.inf)
    logits = jnp.concatenate([ls.reshape(n, nq, h, ks * MOBA_BLOCK), lo], axis=-1)
    p = jax.nn.softmax(logits, axis=-1).astype(v_sel.dtype)
    p_sel = p[..., :ks * MOBA_BLOCK].reshape(n, nq, h, ks, MOBA_BLOCK)
    p_own = p[..., ks * MOBA_BLOCK:]
    o = jnp.einsum('nqhsk,nqhske->nqhe', p_sel, v_sel)
    if shared_own:
        o = o + jnp.einsum('nqhk,nkhe->nqhe', p_own, v_own[:, 0])
    else:
        o = o + jnp.einsum('nqhk,nqkhe->nqhe', p_own, v_own)
    return o

def _moba_prompt(q, k, v, tab_hT):
    n, s, h, e = q.shape
    nb = -(-s // MOBA_BLOCK)
    pad = nb * MOBA_BLOCK - s
    kb = jnp.pad(k, ((0, 0), (0, pad), (0, 0), (0, 0))).reshape(n, nb, MOBA_BLOCK, h, e)
    vb = jnp.pad(v, ((0, 0), (0, pad), (0, 0), (0, 0))).reshape(n, nb, MOBA_BLOCK, h, e)
    kmean = jnp.sum(kb, axis=2, dtype=F32) / MOBA_BLOCK
    ks = min(MOBA_TOP_K, nb)
    nch = s // MOBA_Q_CHUNK
    qch = q.reshape(n, nch, MOBA_Q_CHUNK, h, e).transpose(1, 0, 2, 3, 4)
    ni = jnp.arange(n)[:, None, None, None]
    hi = jnp.arange(h)[None, None, :, None]

    def one_chunk(args):
        qc, c = args
        q_pos = c * MOBA_Q_CHUNK + jnp.arange(MOBA_Q_CHUNK)
        own = q_pos // MOBA_BLOCK
        sel, ok = _moba_route(qc, kmean, own, ks)
        k_sel = kb[ni, sel, :, hi]
        v_sel = vb[ni, sel, :, hi]
        own_blk = (c * MOBA_Q_CHUNK) // MOBA_BLOCK
        k_own = lax.dynamic_index_in_dim(kb, own_blk, axis=1, keepdims=True)
        v_own = lax.dynamic_index_in_dim(vb, own_blk, axis=1, keepdims=True)
        return _moba_attend(qc, q_pos, k_sel, v_sel, sel, ok, k_own, v_own, own, tab_hT)

    o = lax.map(one_chunk, (qch, jnp.arange(nch)))
    return o.transpose(1, 0, 2, 3, 4).reshape(n, s, h, e)

def _moba_sample(q, k_new, v_new, cache_k, cache_v, layer, page_table, tab_hT):
    n, t, h, e = q.shape
    n_pages = page_table.shape[1]
    past = n_pages * PAGE_SIZE
    ppb = MOBA_BLOCK // PAGE_SIZE
    q_pos = past + jnp.arange(t)
    own = q_pos // MOBA_BLOCK
    nbt = -(-(past + t) // MOBA_BLOCK)
    psum = jnp.sum(cache_k[layer, page_table], axis=2, dtype=F32)
    psum = jnp.pad(psum, ((0, 0), (0, nbt * ppb - n_pages), (0, 0), (0, 0)))
    bsum = psum.reshape(n, nbt, ppb, h, e).sum(axis=2).at[:, own].add(k_new.astype(F32))
    kmean = bsum / MOBA_BLOCK
    ks = min(MOBA_TOP_K, nbt)
    sel, ok = _moba_route(q, kmean, own, ks)
    newp = -(-t // PAGE_SIZE)

    def to_pages(a):
        return jnp.pad(a, ((0, 0), (0, newp * PAGE_SIZE - t), (0, 0), (0, 0))).reshape(n, newp, PAGE_SIZE, h, e)

    kp_new, vp_new = to_pages(k_new), to_pages(v_new)
    ni = jnp.arange(n)[:, None, None, None, None]
    hi = jnp.arange(h)[None, None, :, None, None]
    lp = sel[..., None] * ppb + jnp.arange(ppb)
    in_past = (lp < n_pages)[..., None, None]
    phys = page_table[ni, jnp.clip(lp, 0, n_pages - 1)]
    lpn = jnp.clip(lp - n_pages, 0, newp - 1)
    k_sel = jnp.where(in_past, cache_k[layer, phys, :, hi], kp_new[ni, lpn, :, hi]).reshape(n, t, h, ks, MOBA_BLOCK, e)
    v_sel = jnp.where(in_past, cache_v[layer, phys, :, hi], vp_new[ni, lpn, :, hi]).reshape(n, t, h, ks, MOBA_BLOCK, e)
    lpo = own[:, None] * ppb + jnp.arange(ppb)
    in_past_o = (lpo < n_pages)[None, :, :, None, None, None]
    physo = page_table[:, jnp.clip(lpo, 0, n_pages - 1)]
    lpno = jnp.clip(lpo - n_pages, 0, newp - 1)
    k_own = jnp.where(in_past_o, cache_k[layer, physo], kp_new[:, lpno]).reshape(n, t, MOBA_BLOCK, h, e)
    v_own = jnp.where(in_past_o, cache_v[layer, physo], vp_new[:, lpno]).reshape(n, t, MOBA_BLOCK, h, e)
    return _moba_attend(q, q_pos, k_sel, v_sel, sel, ok, k_own, v_own, own, tab_hT)

def _merge(gates, b_conv, b_dil, b_moba, w_out):
    m = gates[..., 0, :] * b_conv + gates[..., 1, :] * b_dil + gates[..., 2, :] * b_moba
    return m @ w_out

def _ffn(x, g, w1, w2):
    h = _rmsnorm(x, g)
    return jnp.square(jax.nn.relu(h @ w1)) @ w2

def _prompt_layer(x, lw, rel_bias):
    (ng, wi, bg, cw, cb, lg, lb, wco, dqn, dkn, wdo, mqn, mkn, wmo, wo, nf, w1, w2) = lw
    n, s, _ = x.shape
    u, dq, dk, dv, mq, mk, mv, gates = _project(x, ng, wi, bg, dqn, dkn, mqn, mkn)
    u_ext = jnp.pad(u, ((0, 0), (CONV_WIDTH - 1, 0), (0, 0)))
    br_conv = _conv_branch(u_ext, cw, cb, lg, lb, wco)
    outs, lses, dil_state = [], [], []
    for g, (win, dil) in enumerate(DIL_GROUPS):
        sl = slice(g * DIL_HPG, (g + 1) * DIL_HPG)
        o, l = _dilated_group_prompt(dq[:, :, sl], dk[:, :, sl], dv[:, :, sl], dil, win // dil, rel_bias[:, sl].T)
        outs.append(o)
        lses.append(l)
        wb = min(win, s)
        dil_state += [dk[:, s - wb:, sl], dv[:, s - wb:, sl]]
    br_dil = _combine_dilated(outs, lses, wdo)
    mo = _moba_prompt(mq, mk, mv, rel_bias[:, DIL_HEADS:].T)
    br_moba = mo.reshape(n, s, MOBA_WIDTH) @ wmo
    x = x + _merge(gates, br_conv, br_dil, br_moba, wo)
    x = x + _ffn(x, nf, w1, w2)
    return x, u[:, s - (CONV_WIDTH - 1):], tuple(dil_state), mk, mv

def _sample_layer(x, conv_buf, dil_bufs, cache_k, cache_v, layer, page_table, lw, rel_bias):
    (ng, wi, bg, cw, cb, lg, lb, wco, dqn, dkn, wdo, mqn, mkn, wmo, wo, nf, w1, w2) = lw
    n, t, _ = x.shape
    u, dq, dk, dv, mq, mk, mv, gates = _project(x, ng, wi, bg, dqn, dkn, mqn, mkn)
    u_ext = jnp.concatenate([conv_buf.astype(u.dtype), u], axis=1)
    br_conv = _conv_branch(u_ext, cw, cb, lg, lb, wco)
    new_conv = u_ext[:, -(CONV_WIDTH - 1):]
    outs, lses, new_bufs = [], [], []
    for g, (win, dil) in enumerate(DIL_GROUPS):
        sl = slice(g * DIL_HPG, (g + 1) * DIL_HPG)
        kbuf, vbuf = dil_bufs[2 * g], dil_bufs[2 * g + 1]
        wb = kbuf.shape[1]
        ke = jnp.concatenate([kbuf.astype(dk.dtype), dk[:, :, sl]], axis=1)
        ve = jnp.concatenate([vbuf.astype(dv.dtype), dv[:, :, sl]], axis=1)
        o, l = _dilated_group_sample(dq[:, :, sl], ke, ve, wb, dil, win // dil, rel_bias[:, sl].T)
        outs.append(o)
        lses.append(l)
        new_bufs += [ke[:, -wb:], ve[:, -wb:]]
    br_dil = _combine_dilated(outs, lses, wdo)
    mo = _moba_sample(mq, mk, mv, cache_k, cache_v, layer, page_table, rel_bias[:, DIL_HEADS:].T)
    br_moba = mo.reshape(n, t, MOBA_WIDTH) @ wmo
    x = x + _merge(gates, br_conv, br_dil, br_moba, wo)
    x = x + _ffn(x, nf, w1, w2)
    return x, new_conv, tuple(new_bufs), mk, mv

def setup_inputs(seed: int = 0) -> dict:
    key = jax.random.key(seed)
    k = jax.random.split(key, 40)
    n_pages = PAST_LEN // PAGE_SIZE
    n_used = DEC_BATCH * n_pages
    n_pool = n_used + n_used // 4

    def nrm(kk, shape, scale):
        return jax.random.normal(kk, shape, F32) * scale

    def gain(kk, shape):
        return 1.0 + nrm(kk, shape, 0.05)

    wb = [min(w, PAST_LEN) for (w, _) in DIL_GROUPS]
    dshape = lambda i: (DEPTH, DEC_BATCH, wb[i], DIL_HPG, DIL_HEAD_DIM)
    page_table = jax.random.permutation(k[11], n_pool)[:n_used].reshape(DEC_BATCH, n_pages).astype(jnp.int32)
    return {
        'x_prompt': nrm(k[0], (BATCH, SEQ, D_MODEL), 1.0),
        'x_sample': nrm(k[1], (DEC_BATCH, DEC_SEQ, D_MODEL), 1.0),
        'state_conv': nrm(k[2], (DEPTH, DEC_BATCH, CONV_WIDTH - 1, CONV_CH), 0.5),
        'state_dil_k0': nrm(k[3], dshape(0), 1.0),
        'state_dil_v0': nrm(k[4], dshape(0), 1.0),
        'state_dil_k1': nrm(k[5], dshape(1), 1.0),
        'state_dil_v1': nrm(k[6], dshape(1), 1.0),
        'state_dil_k2': nrm(k[7], dshape(2), 1.0),
        'state_dil_v2': nrm(k[8], dshape(2), 1.0),
        'cache_k': nrm(k[9], (DEPTH, n_pool, PAGE_SIZE, MOBA_HEADS, MOBA_HEAD_DIM), 1.0),
        'cache_v': nrm(k[10], (DEPTH, n_pool, PAGE_SIZE, MOBA_HEADS, MOBA_HEAD_DIM), 1.0),
        'page_table': page_table,
        'rel_bias': nrm(k[12], (REL_BUCKETS, N_ATT_HEADS), 0.1),
        'norm_mix_g': gain(k[13], (DEPTH, D_MODEL)),
        'w_in': nrm(k[14], (DEPTH, D_MODEL, IN_COLS), D_MODEL ** -0.5),
        'b_gate': nrm(k[15], (DEPTH, N_BRANCH * D_MODEL), 0.02),
        'conv_w': nrm(k[16], (DEPTH, CONV_WIDTH, CONV_CH), CONV_WIDTH ** -0.5),
        'conv_b': nrm(k[17], (DEPTH, CONV_CH), 0.02),
        'conv_ln_g': gain(k[18], (DEPTH, CONV_CH)),
        'conv_ln_b': nrm(k[19], (DEPTH, CONV_CH), 0.02),
        'w_conv_out': nrm(k[20], (DEPTH, CONV_CH, D_MODEL), CONV_CH ** -0.5),
        'dil_qn_g': gain(k[21], (DEPTH, DIL_HEAD_DIM)),
        'dil_kn_g': gain(k[22], (DEPTH, DIL_HEAD_DIM)),
        'w_dil_out': nrm(k[23], (DEPTH, DIL_HPG * DIL_HEAD_DIM, D_MODEL), (DIL_HPG * DIL_HEAD_DIM) ** -0.5),
        'moba_qn_g': gain(k[24], (DEPTH, MOBA_HEAD_DIM)),
        'moba_kn_g': gain(k[25], (DEPTH, MOBA_HEAD_DIM)),
        'w_moba_out': nrm(k[26], (DEPTH, MOBA_WIDTH, D_MODEL), MOBA_WIDTH ** -0.5),
        'w_out': nrm(k[27], (DEPTH, D_MODEL, D_MODEL), D_MODEL ** -0.5),
        'norm_ffn_g': gain(k[28], (DEPTH, D_MODEL)),
        'w_ff1': nrm(k[29], (DEPTH, D_MODEL, FF_HIDDEN), D_MODEL ** -0.5),
        'w_ff2': nrm(k[30], (DEPTH, FF_HIDDEN, D_MODEL), FF_HIDDEN ** -0.5),
    }

def reference(x_prompt, x_sample, state_conv, state_dil_k0, state_dil_v0, state_dil_k1, state_dil_v1,
              state_dil_k2, state_dil_v2, cache_k, cache_v, page_table, rel_bias, norm_mix_g, w_in, b_gate,
              conv_w, conv_b, conv_ln_g, conv_ln_b, w_conv_out, dil_qn_g, dil_kn_g, w_dil_out, moba_qn_g,
              moba_kn_g, w_moba_out, w_out, norm_ffn_g, w_ff1, w_ff2):
    dil_in = (state_dil_k0, state_dil_v0, state_dil_k1, state_dil_v1, state_dil_k2, state_dil_v2)
    xp, xs = x_prompt, x_sample
    conv_p_l, conv_s_l, dil_p_l, dil_s_l = [], [], [], []
    kp_l, vp_l, ks_l, vs_l = [], [], [], []
    for l in range(DEPTH):
        lw = (norm_mix_g[l], w_in[l], b_gate[l], conv_w[l], conv_b[l], conv_ln_g[l], conv_ln_b[l],
              w_conv_out[l], dil_qn_g[l], dil_kn_g[l], w_dil_out[l], moba_qn_g[l], moba_kn_g[l],
              w_moba_out[l], w_out[l], norm_ffn_g[l], w_ff1[l], w_ff2[l])
        xp, cp, dp, kp, vp = _prompt_layer(xp, lw, rel_bias)
        xs, cs, ds, kss, vss = _sample_layer(xs, state_conv[l], tuple(b[l] for b in dil_in), cache_k, cache_v,
                                             l, page_table, lw, rel_bias)
        conv_p_l.append(cp)
        conv_s_l.append(cs)
        dil_p_l.append(dp)
        dil_s_l.append(ds)
        kp_l.append(kp)
        vp_l.append(vp)
        ks_l.append(kss)
        vs_l.append(vss)
    conv_p = jnp.stack(conv_p_l)
    conv_s = jnp.stack(conv_s_l)
    dk0_p, dv0_p, dk1_p, dv1_p, dk2_p, dv2_p = [jnp.stack([d[i] for d in dil_p_l]) for i in range(6)]
    dk0_s, dv0_s, dk1_s, dv1_s, dk2_s, dv2_s = [jnp.stack([d[i] for d in dil_s_l]) for i in range(6)]
    k_p = jnp.stack(kp_l)
    v_p = jnp.stack(vp_l)
    k_s = jnp.stack(ks_l)
    v_s = jnp.stack(vs_l)
    return (xp, xs, conv_p, conv_s, dk0_p, dv0_p, dk1_p, dv1_p, dk2_p, dv2_p,
            dk0_s, dv0_s, dk1_s, dv1_s, dk2_s, dv2_s, k_p, v_p, k_s, v_s)


_drawn_inputs = setup_inputs


def setup_inputs(seed=0):
    import zlib

    import numpy as np

    out = dict(_drawn_inputs(seed))
    spreads = {}
    factors = {'rel_bias': 4.27,
     'b_gate': 8.0,
     'conv_b': 4.479,
     'conv_ln_g': 2.791,
     'conv_ln_b': 8.0,
     'dil_qn_g': 8.0,
     'moba_qn_g': 7.88}
    for name, (base, spread) in spreads.items():
        noise = np.random.default_rng([zlib.crc32(name.encode()), seed]).standard_normal(out[name].shape)
        drawn = base * np.exp(spread * noise) if base else spread * noise
        out[name] = jnp.asarray(drawn.astype(out[name].dtype))
    for name, factor in factors.items():
        out[name] = (out[name] * factor).astype(out[name].dtype)
    return out
```

```python
from contextlib import ExitStack

import concourse.bass as bass
import numpy as np
from concourse import mybir

F32 = mybir.dt.float32
F32R = mybir.dt.float32r
I32 = mybir.dt.int32
U32 = mybir.dt.uint32
ALU = mybir.AluOpType
ACT = mybir.ActivationFunctionType
AX = mybir.AxisListType

P = 128
D = 1024
KD = D // P
SEQ, NS = 256, 8
T = SEQ + NS
C, KC, TAPS = 384, 3, 31
HALO = TAPS - 1
GROUPS = ((128, 1), (512, 4), (2048, 16))
NG, HPG, DH = 3, 4, 32
MH, ME, MW = 4, 64, 256
PAST, PAGE, BLOCK, TOPK = 2048, 128, 256, 3
NB = PAST // BLOCK
ROWS = 16
FF = 4 * D
FT = FF // P
BUCKETS, EXACT, MAXD = 32, 16, 2048
EPS = 1e-6
NEG = -1e30
TW = SEQ + P - 1

CHUNK_ORDER = [5, 6, 2, 3, 4, 1, 0] + list(range(7, 15))
UNITS = [3 * c + k for c in CHUNK_ORDER for k in range(3)]
U_MQ, U_MK, U_MV, U_DQ, U_DK, U_DV, U_B, U_A, U_G = 0, 2, 4, 6, 9, 12, 15, 18, 21
NU = len(UNITS)
Q_UNITS = [0, 1, 6, 7, 8]
QK = [0, 1, 2, 3, 6, 7, 8, 9, 10, 11]

OFF, _n = {}, 0
for _k, _w in (("ident", P), ("eps", 1), ("sub8", 1), ("ones", P), ("bd32", P), ("bd64", P), ("blkT", P), ("blk", NB),
               ("hmask", HPG), ("mmask", 2 * MH), ("iota", NB), ("pick4", MH), ("pick16", 4 * HPG)):
    OFF[_k] = (_n, _n + _w)
    _n += _w
NCONST = _n
NFIRST = P + 2
OH_TOE, OH_MOBA, OH_DIL = 0, TW, TW + PAST
NHOT = TW + PAST + NG * P
POFF, _n = {}, 0
for _k, _w in (("g_mix", KD), ("g_ffn", KD), ("b_gate", 3 * KD), ("conv_w", KC * TAPS), ("conv_b", KC),
               ("ln_g", KC), ("ln_b", KC), ("dqn", 1), ("dkn", 1), ("mqn", 1), ("mkn", 1)):
    POFF[_k] = (_n, _n + _w)
    _n += _w
NPARAM = _n


def bucket(d):
    if d < EXACT:
        return max(int(d), 0)
    big = EXACT + int(np.log(d / EXACT) / np.log(MAXD / EXACT) * (BUCKETS - EXACT) + 1e-9)
    return min(big, BUCKETS - 1)


def shape_constants():
    c = np.zeros((P, NCONST), np.float32)
    p = np.arange(P)

    def put(name, a):
        lo, hi = OFF[name]
        c[:a.shape[0], lo:hi] = a.reshape(a.shape[0], hi - lo)

    put("ident", np.eye(P))
    put("ones", np.ones((P, P)))
    put("bd32", (p[:, None] // DH == p[None] // DH) / DH)
    put("bd64", (p[:, None] // ME == p[None] // ME) / ME)
    put("blkT", np.arange(NB)[:, None] == p[None] // (P // NB))
    put("blk", p[:, None] // (P // NB) == np.arange(NB)[None])
    put("hmask", p[:, None] // DH == np.arange(HPG)[None])
    put("mmask", np.stack([p[:, None] // ME + 2 * t == np.arange(MH)[None] for t in range(2)], 1))
    put("sub8", (p % NS)[:, None])
    put("pick4", p[:, None] % DH == np.arange(MH)[None])
    put("pick16", DH * (np.arange(16) // HPG)[None] + np.arange(16)[None] % HPG == p[:, None])
    put("iota", np.tile(np.arange(NB), (P, 1)))
    put("eps", np.full((P, 1), EPS))
    hot = np.zeros((BUCKETS + 4, NHOT), np.float32)
    for m in range(TW):
        d = 255 - m
        hot[bucket(d), OH_TOE + m] = 1.0
        for g, (w, dil) in enumerate(GROUPS):
            if d < 0 or d % dil or d > w:
                hot[BUCKETS + g, OH_TOE + m] = NEG
        if d < 0:
            hot[BUCKETS + 3, OH_TOE + m] = NEG
    for r in range(ROWS):
        for q in range(P):
            hot[bucket(PAST - ROWS * q - r), OH_MOBA + r * P + q] = 1.0
    for g, (w, dil) in enumerate(GROUPS):
        for i in range(P):
            hot[bucket((P - i) * dil), OH_DIL + g * P + i] = 1.0
    group = np.zeros((4, 16), np.float32)
    for g in range(4):
        group[g, 4 * g:4 * g + 4] = 1.0
    return c, hot, group


def build_layer(nc, A, O):
    base = -(-nc.sbuf_base // 32) * 32
    room = nc.sbuf_usable_end - base
    scratch = nc.dram_tensor("bias_rows", [16, TW], F32).ap()

    with ExitStack() as ctx:
        place = [0]

        def sb(name, shape, dt=F32, at=None):
            size = int(np.prod(shape[1:])) * 4
            off = place[0] if at is None else at
            t = nc.alloc_sbuf_tensor_at(name, shape, dt, offset=base + off)
            end = -(-(off + size) // 32) * 32
            if at is None:
                place[0] = end
            assert end <= room, (name, end, room)
            return t

        def sem(name):
            return ctx.enter_context(nc.semaphore(name))

        xT = sb("xT", [P, KD, T])
        const = sb("const", [P, NCONST])
        param = sb("param", [P, NPARAM])
        sqx = sb("sqx", [P, 2, T])
        rx = sb("rx", [P, T])
        raw_at = place[0]
        raw = [sb(f"raw{s}", [P, 3 * D]) for s in range(3)]
        actT = sb("actT", [P, KD, T])
        second_half = place[0]
        gates_at = place[0]
        gates = sb("gates", [P, 3 * KD, T])
        xnat = sb("xnat", [P, 3, D], at=gates_at)
        hot = sb("hot", [BUCKETS + 4, NHOT], at=gates_at + 3 * D * 4)
        qkv = sb("qkv", [P, 15, T])
        uext = sb("uext", [P, KC, HALO + SEQ])
        usx = sb("usx", [P, KC, NS, TAPS])
        ca = sb("ca", [P, KC, T])
        cb = sb("cb", [P, KC, T])
        csq = sb("csq", [P, KC, T])
        cact = sb("cact", [P, KC, T])
        oT = sb("oT", [P, 3, T])
        vnat = sb("vnat", [P, 2, 640])
        snat = sb("snat", [NS, 2304])
        unat = sb("unat", [HALO, C])
        ebias = sb("ebias", [P, 2, 4, 256])
        logits_at = place[0]
        logits = sb("logits", [P, 1536])
        knat = sb("knat", [P, 2, 640], at=logits_at)
        probT_at = place[0]
        probT = sb("probT", [P, 1536])
        kv_at = place[0]
        kv = [sb(f"kv{s}", [P, ROWS * MW]) for s in range(2)]
        stk = sb("stk", [P, NG, NS, P], at=kv_at)
        stv = sb("stv", [P, NG, NS, P], at=kv_at + ROWS * MW * 4)
        sqq = sb("sqq", [P, 2, T])
        stdq = sb("stdq", [P, 4, T])
        rq = sb("rq", [P, T])
        scv = sb("scv", [NS * HALO // 2, 2, C], at=probT_at)
        trow = sb("trow", [16, TW], at=gates_at + 3 * D * 4 + NHOT * 4 + 4)
        tab = sb("tab", [BUCKETS + 4, 16])
        bias = sb("bias", [P, 92])
        ptab = sb("ptab", [P, NS], I32)
        pidx = sb("pidx", [P, NS], I32)
        smp = sb("sm", [P, NS * ROWS * MH + DH - MH])
        sm = smp[:, 0:NS * ROWS * MH].rearrange("p (n c) -> p n c", n=NS)
        sdp = sb("sd", [P, NG * 32 + DH - HPG])
        sd = sdp[:, 0:NG * 32]
        vo = sb("vo", [P, MW])
        pnd = sb("pnd", [P, NG, NS])
        pnm = sb("pnm", [P, 2, NS])
        rnd = sb("rnd", [P, NG * NS, HPG])
        rnm = sb("rnm", [P, 2, NS, MH])
        ln = sb("ln", [P, 128])
        rt = sb("rt", [P, 32])
        r32 = sb("r32", [32, NB])
        top = sb("top", [32, 8])
        topi = sb("topi", [32, 8], U32)
        topf = sb("topf", [32, 8])
        selb = sb("selb", [32, NB])
        selT = sb("selT", [NB, 32])
        mc = sb("mc", [P, 64])
        mm = sb("mm", [64, 1])
        dg = sb("dg", [64, 64])
        lmax = sb("lmax", [P, 32])
        gmx = sb("gmx", [P, 64])
        ssum = sb("ssum", [P, 64])
        rden = sb("rden", [P, 64])
        t1 = sb("t1", [P, NG, 32])
        t2 = sb("t2", [P, 2, 32])
        nmax = sb("nmax", [P, 4])
        psum_ = sb("psum_", [P, 4])
        pinv = sb("pinv", [P, 4])
        xs = sb("xs", [P, 3, D], at=logits_at)
        ssx = sb("ssx", [P, 8])
        mtmp = sb("mtmp", [P, 3, T], at=logits_at)
        place[0] = second_half
        hs = [sb(f"hs{k}", [P, KD, T], F32R) for k in range(2)]
        as_ = [sb(f"as{k}", [P, FT, T], F32R) for k in range(2)]
        ws = [[sb(f"ws{k}_{s}", [P, KD, P], F32R) for s in range(4)] for k in range(2)]
        rinv = sb("rinv", [P, T])
        rl = sb("rl", [P, 2, T])
        ra = sb("ra", [P, 2, T])
        yT = sb("yT", [P, 2, T])
        ynat = sb("ynat", [P, 3 * KD, P])
        fraw = [sb(f"fraw{s}", [P, 2 * D], at=raw_at + (3 + s) % 4 * 2 * D * 4) for s in range(4)]

        ps = ctx.enter_context(nc.psum_tensor("ps", [P, 8, 512], F32))

        def cst(name, rows=P):
            return const[0:rows, OFF[name][0]:OFF[name][1]]

        def par(name, k=0):
            return param[:, POFF[name][0] + k:POFF[name][0] + k + 1]

        ident, ones = cst("ident"), cst("ones")
        ps_s1 = ps[:, 3:5, :].rearrange("p a b -> p (a b)")

        first_in, const_in, hot_in, small_in, state_in = (sem(n) for n in
                                                          ("first_in", "const_in", "hot_in", "small_in", "state_in"))
        x_in = [sem(f"x_in{t}") for t in range(3)]
        w_in = [sem(f"w_in{s}") for s in range(3)]
        kv_in = [sem(f"kv_in{s}") for s in range(2)]
        e_in = [sem(f"e_in{s}") for s in range(2)]
        fw_in = [sem(f"fw_in{s}") for s in range(4)]
        rows_out = sem("rows_out")
        stored, copied, y_stored = sem("stored"), sem("copied"), sem("y_stored")
        x_squared, x_std, x_scaled, h_turned, h_ready, x_turned, x_copied = (sem(n) for n in (
            "x_squared", "x_std", "x_scaled", "h_turned", "h_ready", "x_turned", "x_copied"))
        rows_made, bias_made, bias_copied = sem("rows_made"), sem("bias_made"), sem("bias_copied")
        idx_ready = sem("idx_ready")
        z_done, z_evac = sem("z_done"), sem("z_evac")
        sq_ready, ms_done, std_done, qn_done = sem("sq_ready"), sem("ms_done"), sem("std_done"), sem("qn_done")
        nat_done, nat_evac = sem("nat_done"), sem("nat_evac")
        qb_done, prod_done, kred_done = sem("qb_done"), sem("prod_done"), sem("kred_done")
        padded, u_ready, conv_done = sem("padded"), sem("u_ready"), sem("conv_done")
        conv_step = sem("conv_step")
        dve = sem("dve_step")
        act = sem("act_step")
        new_ready, new_dot, new_read = sem("new_ready"), sem("new_dot"), sem("new_read")
        route_ready, route_dot, sel_ready, sel_turned, selT_ready, sel_spread, sel_read = (sem(n) for n in (
            "route_ready", "route_dot", "sel_ready", "sel_turned", "selT_ready", "sel_spread", "sel_read"))
        mc_ready, mc_turned, dg_ready, max_spread, sub_ready, exp_done, sum_ready, den_dot, den_read = (
            sem(n) for n in ("mc_ready", "mc_turned", "dg_ready", "max_spread", "sub_ready", "exp_done",
                             "sum_ready", "den_dot", "den_read"))
        pvd_done, pvm_done, so_ready = sem("pvd_done"), sem("pvm_done"), sem("so_ready")
        vo_ready, vt_done = sem("vo_ready"), sem("vt_done")
        mean_done, xc_ready, csq_ready, var_done, cstd, cy_ready, cyn, csg, cact_ready = (sem(n) for n in (
            "mean_done", "xc_ready", "csq_ready", "var_done", "cstd", "cy_ready", "cyn", "csg", "cact_ready"))
        score_done, l_ready, p_exp, p_ready, pt_done, pt_evac, o_done, o_evac = (sem(n) for n in (
            "score_done", "l_ready", "p_exp", "p_ready", "pt_done", "pt_evac", "o_done", "o_evac"))
        gate_ready, br_done, br_read, m_ready = sem("gate_ready"), sem("br_done"), sem("br_read"), sem("m_ready")
        wo_done, x1_ready, x1_squared, x1_summed, x1_std = (sem(n) for n in (
            "wo_done", "x1_ready", "x1_squared", "x1_summed", "x1_std"))
        h_hi, h_lo = sem("h_hi"), sem("h_lo")
        hi_ready, lo_ready, ff_done, bank_free = (sem(n) for n in (
            "hi_ready", "lo_ready", "ff_done", "bank_free"))
        ahi_ready, ra_ready, a_ready = sem("ahi_ready"), sem("ra_ready"), sem("a_ready")
        y_done, y_added, y_turned, y_evac = sem("y_done"), sem("y_added"), sem("y_turned"), sem("y_evac")

        w_in_v = A["w_in"].rearrange("l (k p) n -> p (l k) n", p=P)
        w_co = A["w_conv_out"].rearrange("l (k p) n -> p (l k) n", p=P)
        w_do = A["w_dil_out"].rearrange("l (k p) n -> p (l k) n", p=P)
        w_mo = A["w_moba_out"].rearrange("l (k p) n -> p (l k) n", p=P)
        w_o = A["w_out"].rearrange("l (k p) n -> p (l k) n", p=P)
        w1_v = A["w_ff1"].rearrange("l (k p) n -> p (l k) n", p=P)
        w2_v = A["w_ff2"].rearrange("l (k p) n -> p (l k) n", p=P)
        NCH = 20
        BR0, BR1, WO0 = 15, 16, 17
        parts = [1] * 16 + [2] + [1] * 3
        arrived = [16 * sum(parts[k] for k in range(c % 3, c + 1, 3)) for c in range(NCH)]

        def raw3(c):
            return raw[c % 3][:, :].rearrange("p (k n) -> p k n", n=C)

        def rawb(c):
            return raw[c % 3][:, :].rearrange("p (k n) -> p k n", n=D)

        NAT = ([("q", U_MQ + t, 384 + P * t) for t in range(2)] + [("k", U_MK + t, 384 + P * t) for t in range(2)]
               + [("v", U_MV + t, 384 + P * t) for t in range(2)] + [("q", U_DQ + t, P * t) for t in range(3)]
               + [("k", U_DK + t, P * t) for t in range(3)] + [("v", U_DV + t, P * t) for t in range(3)]
               + [("s", t, 0) for t in range(3)] + [("u", t, P * t) for t in range(3)])
        N_Q, N_V, N_S, N_U = 9, 15, 18, 21

        kv_parts = [1] * 8 + [3, 3] + [1] * 8
        kv_arrived = [16 * sum(kv_parts[k] for k in range(s % 2, s + 1, 2)) for s in range(18)]
        IT_SK, IT_SV, IT_V = 8, 9, 10

        s_d, s_m = DH ** -0.5, ME ** -0.5
        state = [(A[f"state_dil_k{g}"], A[f"state_dil_v{g}"], O[f"dk{g}_s"], O[f"dv{g}_s"]) for g in range(3)]

        def weights1(slot, u):
            return fraw[slot][:, :].rearrange("p (k n) -> p k n", n=2 * P)[:, :, u * P:(u + 1) * P]

        def weights2(slot, u):
            return fraw[slot][:, u * D:(u + 1) * D].rearrange("p (k n) -> p k n", n=P)

        block = ctx.enter_context(nc.Block())

        def reversed_tiles(ap):
            return ap.rearrange("p (t c) -> p t c", c=P)[:, :, ::-1]

        def load_bias(eng, h):
            src = bass.AP(scratch.tensor, h * TW, [[1, P], [HPG * TW, 4], [1, 256]])
            eng.dma_start(ebias[:, h % 2], src).then_inc(e_in[h % 2], 16)

        @block.sync
        def _(sp):
            xp = A["x_prompt"].rearrange("b (t p) d -> p (b t) d", p=P)
            sp.dma_start(xnat[0:NS, 2, :], A["x_sample"].rearrange("b t d -> (b t) d")).then_inc(x_in[2], 16)
            for t in range(2):
                sp.dma_start(xnat[:, t], xp[:, t]).then_inc(x_in[t], 16)

            def load(c):
                if c >= 3:
                    last = c - 3
                    if last < 15:
                        sp.wait_ge(z_done, 3 * last + 3)
                    elif last < WO0:
                        sp.wait_ge(br_done, KD)
                if c < 15:
                    k = CHUNK_ORDER[c]
                    sp.dma_start(raw3(c), w_in_v[:, :, k * C:(k + 1) * C]).then_inc(w_in[c % 3], 16)
                elif c == BR0:
                    sp.dma_start(rawb(c), w_co).then_inc(w_in[c % 3], 16)
                elif c == BR1:
                    sp.dma_start(rawb(c)[:, 0:1, :], w_do).then_inc(w_in[c % 3], 16)
                    sp.dma_start(rawb(c)[:, 1:3, :], w_mo).then_inc(w_in[c % 3], 16)
                else:
                    k = c - WO0
                    n = min(C, D - k * C)
                    sp.dma_start(raw3(c)[:, :, 0:n], w_o[:, :, k * C:k * C + n]).then_inc(w_in[c % 3], 16)

            for c in range(NCH - 2):
                load(c)
                if c == 2:
                    sp.wait_ge(rows_made, 1)
                    sp.dma_start(scratch, trow[:, :]).then_inc(rows_out, 16)
                    sp.wait_ge(rows_out, 16)
                    for h in range(2):
                        load_bias(sp, h)
                if c == 11:
                    sp.wait_ge(nat_evac, N_V)
                    for g, (w, _) in enumerate(GROUPS):
                        t0 = 0 if w > P else 1
                        for src, o in ((knat, O[f"dk{g}_p"]), (vnat, O[f"dv{g}_p"])):
                            sp.dma_start(o.rearrange("l b (t p) h e -> p (l b t) (h e)", p=P),
                                         src[:, t0:2, g * P:(g + 1) * P]).then_inc(stored, 16)
                        for col, o in ((640, O[f"dk{g}_s"]), (1280, O[f"dv{g}_s"])):
                            r = o.rearrange("l n w h e -> (l n) w (h e)")
                            sp.dma_start(r[:, w - 1, :], snat[:, col + g * P:col + (g + 1) * P]).then_inc(stored, 16)
                    for src, o in ((knat, O["k_p"]), (vnat, O["v_p"])):
                        sp.dma_start(o.rearrange("l b (t p) h e -> p (l b t) (h e)", p=P),
                                     src[:, :, 384:640]).then_inc(stored, 16)
                    for col, o in ((640, O["k_s"]), (1280, O["v_s"])):
                        sp.dma_start(o.rearrange("l n t h e -> (l n t) (h e)"),
                                     snat[:, col + 384:col + 640]).then_inc(stored, 16)
                if c in (16, 17):
                    sp.wait_ge(l_ready, c - 15)
                    load_bias(sp, c - 14)
                if c == 13:
                    sp.wait_ge(nat_evac, N_U)
                    sp.dma_start(O["conv_p"].rearrange("l b t c -> (l b t) c"), unat[:, :]).then_inc(stored, 16)
                    o = O["conv_s"].rearrange("l n t c -> (l n) t c")
                    sp.dma_start(o[:, HALO - 1, :], snat[:, 1920:2304]).then_inc(stored, 16)
                    sp.dma_start(o[:, 0:HALO - 1, :],
                                 A["state_conv"].rearrange("l n t c -> (l n) t c")[:, 1:HALO, :]).then_inc(stored, 16)
            load(NCH - 2)
            load(NCH - 1)

            def load_ff(i, s, second):
                if second:
                    c = i * 4 + s
                    src = w2_v[:, (s % 2) * 16:(s % 2) * 16 + 16, bass.ds(i * 256 + (s // 2) * P, P)]
                    sp.dma_start(fraw[s][:, :].rearrange("p (k n) -> p k n", n=P), src).then_inc(fw_in[s], 16)
                else:
                    src = w1_v[:, :, bass.ds(i * 1024 + s * 256, 256)]
                    sp.dma_start(fraw[s][:, :].rearrange("p (k n) -> p k n", n=256), src).then_inc(fw_in[s], 16)

            def copy_state(n):
                for g in (1, 2):
                    w = GROUPS[g][0]
                    for src, dst in ((state[g][0], state[g][2]), (state[g][1], state[g][3])):
                        a = src.rearrange("l n w h e -> (l n) (w h e)")[bass.ds(n, 1), P:w * P]
                        b = dst.rearrange("l n w h e -> (l n) (w h e)")[bass.ds(n, 1), 0:(w - 1) * P]
                        sp.dma_start(b, a).then_inc(copied, 16)

            for s in range(4):
                sp.wait_ge(wo_done, (3, 6, 8, 8)[s])
                load_ff(0, s, False)
            copy_state(0)
            with sp.Fori(1, 4) as i:
                for s in range(4):
                    sp.wait_ge(lo_ready, i * 8 + 2 * s - 6)
                    load_ff(i, s, False)
                copy_state(i)
            with sp.Fori(0, 4) as i:
                for s in range(4):
                    sp.wait_ge(lo_ready, i * 8 + 32 + 2 * s - 6)
                    load_ff(i, s, True)
                copy_state(i + 4)
            for src, dst in ((state[0][0], state[0][2]), (state[0][1], state[0][3])):
                a = src.rearrange("l n w h e -> (l n) (w h e)")[:, P:P * P]
                b = dst.rearrange("l n w h e -> (l n) (w h e)")[:, 0:(P - 1) * P]
                sp.dma_start(b, a).then_inc(copied, 16)
            sp.wait_ge(stored, 16 * (12 + 4 + 3))
            sp.wait_ge(copied, 16 * (4 * NS + 2))

        @block.gpsimd
        def _(pool):
            pool.memset(uext[:, :, 0:HALO], 0.0).then_inc(padded, 1)
            pool.memset(smp[:, NS * ROWS * MH:], 0.0).then_inc(padded, 1)
            pool.memset(sdp[:, NG * 32:], 0.0).then_inc(padded, 1)
            pool.wait_ge(idx_ready, 1)
            pages = [A[k].rearrange("l n (c r) h e -> (l n c) (r h e)", r=ROWS) for k in ("cache_k", "cache_v")]
            for s in range(18):
                if 2 <= s <= IT_SV:
                    pool.wait_ge(kred_done, s - 1)
                elif s == IT_V:
                    pool.wait_ge(kred_done, IT_SK + 1)
                elif s == IT_V + 1:
                    pool.wait_ge(pvd_done, 1)
                elif s > IT_V + 1:
                    pool.wait_ge(pvm_done, s - IT_V - 1)
                if s in (IT_SK, IT_SV):
                    dst = stk if s == IT_SK else stv
                    for g, (w, dil) in enumerate(GROUPS):
                        src = state[g][0 if s == IT_SK else 1].rearrange("l n (i d) h e -> i d (l n) (h e)", d=dil)
                        pool.dma_start(dst[:, g], src[:, 0]).then_inc(kv_in[s % 2], 16)
                else:
                    n = s if s < IT_SK else s - IT_V
                    pool.indirect_dma_start(kv[s % 2][:, :], None, pages[s >= IT_V],
                                            bass.IndirectOffsetOnAxis(ap=pidx[:, n:n + 1], axis=0)
                                            ).then_inc(kv_in[s % 2], 16)

            yp = O["y_prompt"].rearrange("b (t p) d -> p (b t) d", p=P)
            ys = O["y_sample"].rearrange("b t d -> (b t) d")
            with pool.Fori(0, KD) as m:
                pool.wait_ge(y_evac, m + 1)
                pool.dma_start(yp[:, :, bass.ds(m * P, P)], ynat[:, bass.ds(m * 3, 2), :]).then_inc(y_stored, 16)
                pool.dma_start(ys[:, bass.ds(m * P, P)], ynat[0:NS, bass.ds(m * 3 + 2, 1), :].rearrange(
                    "p a b -> p (a b)")).then_inc(y_stored, 16)
            pool.wait_ge(y_stored, 16 * 2 * KD)

        @block.tensor
        def _(pe):
            def turn_h():
                pe.wait_ge(first_in, 16)
                pe.wait_ge(x_scaled, 3)
                for i in range(KD):
                    if i >= 4:
                        pe.wait_ge(h_ready, i - 3)
                    for t, n in ((0, P), (1, P), (2, NS)):
                        ins = pe.transpose(ps[:, 4 + i % 4, t * P:t * P + n], xs[0:n, t, i * P:(i + 1) * P],
                                           ident[0:n, 0:n])
                    ins.then_inc(h_turned, 1)

            def turn_x(i):
                if i >= 2:
                    pe.wait_ge(x_copied, i - 1)
                bank = 2 + i % 2
                if i < 2:
                    pe.wait_ge(bias_copied, 2)
                for t, n in ((0, P), (1, P), (2, NS)):
                    ins = pe.transpose(ps[:, bank, t * P:t * P + n], xnat[0:n, t, i * P:(i + 1) * P], ident[0:n, 0:n])
                ins.then_inc(x_turned, 1)

            def bias_tables():
                pe.wait_ge(const_in, 16)
                pe.wait_ge(hot_in, 48)
                pe.matmul(ps[0:16, 2, 0:TW], tab[:, :], hot[:, OH_TOE:OH_TOE + TW],
                          start=True, stop=True).then_inc(bias_made, 1)
                for r in range(ROWS):
                    pe.matmul(ps[:, 3, r * 4:r * 4 + 4], hot[0:BUCKETS, OH_MOBA + r * P:OH_MOBA + (r + 1) * P],
                              tab[0:BUCKETS, 12:16], start=True, stop=True)
                for g in range(NG):
                    pe.matmul(ps[:, 3, 64 + g * 4:68 + g * 4], hot[0:BUCKETS, OH_DIL + g * P:OH_DIL + (g + 1) * P],
                              tab[0:BUCKETS, 4 * g:4 * g + 4], start=True, stop=True)
                pe.matmul(ps[:, 3, 76:92], ones[0:1, :], tab[0:1, :], start=True, stop=True).then_inc(bias_made, 1)

            def unit(j):
                c = j // 3
                pe.wait_ge(w_in[c % 3], arrived[c])
                if j >= 2:
                    pe.wait_ge(z_evac, j - 1)
                col = (j % 3) * P
                for k in range(KD):
                    if j == 0:
                        pe.wait_ge(h_ready, k + 1)
                    ins = pe.matmul(ps[:, j % 2, 0:T], raw3(c)[:, k, col:col + P], actT[:, k],
                                    start=k == 0, stop=k == KD - 1)
                ins.then_inc(z_done, 1)

            def mean_square(q):
                pe.wait_ge(sq_ready, q + 1)
                if q >= 2:
                    pe.wait_ge(std_done, q - 1)
                bd = cst("bd64") if q < 4 else cst("bd32")
                pe.matmul(ps[:, 6 + q % 2, 0:T], bd, sqq[:, q % 2], start=True, stop=True).then_inc(ms_done, 1)

            def natural(i):
                kind, u, _ = NAT[i]
                bank = 2 + i % 2
                if i < 2:
                    pe.wait_ge(x_copied, KD)
                else:
                    pe.wait_ge(nat_evac, i - 1)
                if kind in "qk":
                    pe.wait_ge(qn_done, QK.index(u) + 1)
                elif kind == "v":
                    pe.wait_ge(z_evac, u + 1)
                if kind in "kv":
                    for t in range(2):
                        pe.transpose(ps[:, bank, t * P:(t + 1) * P], qkv[:, u, t * P:(t + 1) * P], ident)
                if kind in "qkv":
                    ins = pe.transpose(ps[0:NS, bank, 256:384], qkv[:, u, SEQ:T], ident)
                elif kind == "s":
                    pe.wait_ge(state_in, 16)
                    for t in range(2):
                        ins = pe.transpose(ps[:, bank, t * 120:(t + 1) * 120], scv[:, t, u * P:(u + 1) * P],
                                           ident[0:120, 0:120])
                else:
                    pe.wait_ge(u_ready, 2)
                    pe.transpose(ps[0:HALO, bank, 0:P], uext[:, u, SEQ:SEQ + HALO], ident)
                    ins = pe.transpose(ps[0:NS, bank, 256:384], usx[:, u, :, HALO], ident)
                ins.then_inc(nat_done, 1)

            def spread_query(n):
                pe.wait_ge(nat_evac, 2 if n < NS else N_Q)
                if n >= 2:
                    pe.wait_ge(prod_done, n - 1)
                lo, hi = (384, 640) if n < NS else (0, 384)
                sel = ident[0:NS, n % NS:n % NS + 1].broadcast_to([NS, P])
                pe.matmul(ps[:, 4 + n % 2, 0:hi - lo], sel, snat[:, lo:hi], start=True, stop=True).then_inc(qb_done, 1)

            def new_logits():
                pe.wait_ge(new_ready, 2)
                pe.wait_ge(std_done, len(QK))
                pe.matmul(ps[:, 7, 0:96], ones, rnd[:, :, :].rearrange("p a b -> p (a b)"), start=True, stop=True)
                for t in range(2):
                    ins = pe.matmul(ps[:, 7, 96:128], ones, rnm[:, t].rearrange("p a b -> p (a b)"),
                                    start=t == 0, stop=t == 1)
                ins.then_inc(new_dot, 1)

            def route():
                pe.wait_ge(route_ready, 1)
                pe.wait_ge(new_read, 4)
                pe.matmul(ps[0:32, 7, 128:136], rt[:, :], cst("blk"), start=True, stop=True).then_inc(route_dot, 1)

            def turn_selection():
                pe.wait_ge(sel_ready, 1)
                pe.transpose(ps[0:NB, 7, 136:168], selb[:, :], ident[0:32, 0:32]).then_inc(sel_turned, 1)

            def spread_selection():
                pe.wait_ge(selT_ready, 1)
                pe.matmul(ps[:, 7, 168:200], cst("blkT", NB), selT[:, :], start=True, stop=True).then_inc(sel_spread, 1)

            def turn_max():
                pe.wait_ge(sel_read, 1)
                pe.wait_ge(mc_ready, 2)
                pe.transpose(ps[0:64, 7, 200:328], mc[:, :], ident).then_inc(mc_turned, 1)

            def spread_max():
                pe.wait_ge(dg_ready, 1)
                pe.matmul(ps[:, 7, 328:392], ones[0:64, :], dg[:, :], start=True, stop=True).then_inc(max_spread, 1)

            def denominators():
                pe.wait_ge(sum_ready, 2)
                pe.matmul(ps[:, 7, 392:456], ones, ssum[:, :], start=True, stop=True).then_inc(den_dot, 1)

            def values_dilated():
                pe.wait_ge(den_read, 1)
                pe.wait_ge(exp_done, 3)
                pe.wait_ge(padded, 3)
                pe.wait_ge(kv_in[1], kv_arrived[IT_SV])
                for half in range(2):
                    for g in range(NG):
                        for j in range(4):
                            n = 4 * half + j
                            ins = pe.matmul(ps[j * DH:(j + 1) * DH, 7, 256 + half * P:256 + (half + 1) * P],
                                            sdp[:, g * 32 + 4 * n:g * 32 + 4 * n + DH], stv[:, g, n],
                                            start=g == 0, stop=g == NG - 1, tile_position=(0, j * DH))
                ins.then_inc(pvd_done, 1)

            def turn_dilated():
                pe.wait_ge(vo_ready, 1)
                for half in range(2):
                    ins = pe.matmul(ps[:, 7, 64 + 16 * half:80 + 16 * half], vo[:, half * P:(half + 1) * P], cst("pick16"),
                                    start=True, stop=True)
                ins.then_inc(vt_done, 1)

            def values_moba(n):
                it = IT_V + n
                pe.wait_ge(kv_in[it % 2], kv_arrived[it])
                pe.wait_ge(vo_ready, n + 1)
                vv = kv[it % 2][:, :].rearrange("p (r c) -> p r c", c=MW)
                for r in range(ROWS):
                    j = r % 4
                    ins = pe.matmul(ps[j * DH:(j + 1) * DH, 7, 256:512],
                                    smp[:, n * ROWS * MH + MH * r:n * ROWS * MH + MH * r + DH], vv[:, r],
                                    start=r < 4, stop=r >= ROWS - 4, tile_position=(0, j * DH))
                ins.then_inc(pvm_done, 1)

            def turn_moba(n):
                pe.wait_ge(vo_ready, n + 2)
                for t in range(2):
                    ins = pe.matmul(ps[:, 7, t * 32 + 4 * n:t * 32 + 4 * n + 4], vo[:, t * P:(t + 1) * P], cst("pick4"),
                                    start=True, stop=True)
                ins.then_inc(vt_done, 1)

            def conv_mean():
                pe.wait_ge(conv_done, 1)
                pe.wait_ge(nat_evac, N_U)
                for t in range(KC):
                    ins = pe.matmul(ps[:, 2, 0:T], ones, ca[:, t], start=t == 0, stop=t == KC - 1)
                ins.then_inc(mean_done, 1)

            def conv_var():
                pe.wait_ge(csq_ready, 1)
                for t in range(KC):
                    ins = pe.matmul(ps[:, 3, 0:T], ones, csq[:, t], start=t == 0, stop=t == KC - 1)
                ins.then_inc(var_done, 1)

            def scores(h):
                if h == 0:
                    pe.wait_ge(prod_done, 2 * NS)
                    pe.wait_ge(cstd, 1)
                else:
                    pe.wait_ge(pt_evac, 3 * h)
                r = slice(h * DH, (h + 1) * DH)
                for g in range(NG):
                    pe.matmul(ps[:, 2, g * P:(g + 1) * P], qkv[r, U_DQ + g, 0:P], qkv[r, U_DK + g, 0:P],
                              start=True, stop=True)
                for g in range(NG):
                    pe.matmul(ps_s1[:, g * 256:(g + 1) * 256], qkv[r, U_DQ + g, P:SEQ], qkv[r, U_DK + g, 0:SEQ],
                              start=True, stop=True)
                r = slice(h % 2 * ME, (h % 2 + 1) * ME)
                pe.matmul(ps[:, 5, 0:P], qkv[r, U_MQ + h // 2, 0:P], qkv[r, U_MK + h // 2, 0:P], start=True, stop=True)
                pe.matmul(ps[:, 5, P:384], qkv[r, U_MQ + h // 2, P:SEQ], qkv[r, U_MK + h // 2, 0:SEQ],
                          start=True, stop=True).then_inc(score_done, 1)

            def turn_probs(h):
                pe.wait_ge(p_ready, 4 * (h + 1))
                for b in range(12):
                    ins = pe.transpose(ps[:, 2 + b // 4, (b % 4) * P:(b % 4 + 1) * P], logits[:, b * P:(b + 1) * P], ident)
                    if b % 4 == 3:
                        ins.then_inc(pt_done, 1)

            def values_prompt(h):
                pe.wait_ge(pt_evac, 3 * (h + 1))
                if h >= 1:
                    pe.wait_ge(o_evac, 2 * h)

                def run(out, steps):
                    for k, (lhsT, b) in enumerate(steps):
                        ins = pe.matmul(out, lhsT, probT[:, b * P:(b + 1) * P], start=k == 0, stop=k == len(steps) - 1)
                    return ins

                out = ps[h * DH:(h + 1) * DH, 6, :]
                v = [[vnat[:, t, g * P + h * DH:g * P + (h + 1) * DH] for t in range(2)] for g in range(NG)]
                run(out[:, 0:P], [(v[g][0], g) for g in range(NG)])
                run(out[:, P:256], [(v[g][t], 3 + 2 * g + t) for g in range(NG) for t in range(2)])
                out = ps[h % 2 * ME:(h % 2 + 1) * ME, 6, :]
                v = [vnat[:, t, 384 + h * ME:384 + (h + 1) * ME] for t in range(2)]
                run(out[:, 256:384], [(v[0], 9)])
                run(out[:, 384:512], [(v[t], 10 + t) for t in range(2)]).then_inc(o_done, 1)

            def branches(i):
                if i == 0:
                    pe.wait_ge(cact_ready, 1)
                    pe.wait_ge(so_ready, 2)
                    pe.wait_ge(o_evac, 8)
                    pe.wait_ge(z_evac, NU)
                    pe.wait_ge(w_in[BR0 % 3], arrived[BR0])
                    pe.wait_ge(w_in[BR1 % 3], arrived[BR1])
                if i >= 2:
                    pe.wait_ge(br_read, i - 1)
                b0 = 3 * (i % 2)
                cols = slice(i * P, (i + 1) * P)
                for t in range(KC):
                    pe.matmul(ps[:, b0, 0:T], rawb(BR0)[:, t, cols], cact[:, t], start=t == 0, stop=t == KC - 1)
                pe.matmul(ps[:, b0 + 1, 0:T], rawb(BR1)[:, 0, cols], oT[:, 0], start=True, stop=True)
                for t in range(2):
                    ins = pe.matmul(ps[:, b0 + 2, 0:T], rawb(BR1)[:, 1 + t, cols], oT[:, 1 + t], start=t == 0, stop=t == 1)
                ins.then_inc(br_done, 1)

            def project_out(i):
                c = WO0 + i // 3
                pe.wait_ge(w_in[c % 3], arrived[c])
                pe.wait_ge(m_ready, KD)
                if i >= 2:
                    pe.wait_ge(x1_ready, i - 1)
                for k in range(KD):
                    ins = pe.matmul(ps[:, 6 + i % 2, 0:T], raw3(c)[:, k, (i % 3) * P:(i % 3 + 1) * P], actT[:, k],
                                    start=k == 0, stop=k == KD - 1)
                ins.then_inc(wo_done, 1)

            def sum_x1(i):
                pe.wait_ge(x1_squared, i + 1)
                if i == 0:
                    pe.wait_ge(br_read, KD)
                pe.matmul(ps[:, 0, 0:T], ones, sqx[:, i % 2], start=i == 0, stop=i == KD - 1).then_inc(x1_summed, 1)

            turn_h()
            for j in range(NU):
                unit(j)
                if j == 1:
                    bias_tables()
                if j in (2, 3):
                    for i in range(4):
                        turn_x(4 * (j - 2) + i)
                if 1 <= j <= 4:
                    mean_square(j - 1)
                if 7 <= j <= 12:
                    mean_square(j - 3)
                for i in {4: (0, 1), 5: (2, 3), 6: (4,), 7: (5,), 11: (6,), 13: (7, 8), 16: (9, 10), 18: (11, 12),
                          19: (13,), 20: (14,), 21: (15,), 22: (16,), 23: (17,), 26: (18, 19, 20)}.get(j, ()):
                    natural(i)
                for n in {5: (0, 1), 8: (2,), 10: (3,), 12: (4,), 15: (5,), 17: (6,), 19: (7,), 21: (8,),
                          22: (9,), 24: (10, 11), 25: (12, 13, 14, 15)}.get(j, ()):
                    spread_query(n)
                if j == 23:
                    new_logits()
                if j == 27:
                    route()
                if j == 28:
                    turn_selection()
                if j == 29:
                    spread_selection()
                if j == 30:
                    turn_max()
                if j == 31:
                    spread_max()
                if j == 32:
                    denominators()
                if j == 33:
                    values_dilated()
                if j == 34:
                    conv_mean()
                if j == 35:
                    conv_var()
                if j in (36, 39, 42):
                    scores((j - 36) // 3)
                if j in (38, 41, 44):
                    turn_probs((j - 38) // 3)
                if j in (39, 42):
                    values_prompt((j - 39) // 3)
                if j == 34:
                    turn_dilated()
                if 36 < j:
                    turn_moba(j - 37)
                if 36 <= j < 44:
                    values_moba(j - 36)
            values_prompt(2)
            scores(3)
            turn_probs(3)
            values_prompt(3)
            for i in range(KD):
                branches(i)
            pe.sem_inc(ff_done, 4)
            for i in range(KD):
                project_out(i)
                if i >= 1:
                    sum_x1(i - 1)
            sum_x1(KD - 1)

            def product(bank, s, rhs, first, last):
                for k in range(KD):
                    for a, b in ((0, 0), (0, 1), (1, 0)):
                        ins = pe.matmul(ps[:, bank, 0:T], ws[a][s][:, k], rhs[b][k],
                                        start=first and k == 0 and (a, b) == (0, 0),
                                        stop=last and k == KD - 1 and (a, b) == (1, 0))
                return ins

            pe.wait_ge(h_hi, KD)
            pe.wait_ge(h_lo, KD)
            with pe.Fori(0, 4) as i:
                for u in range(8):
                    pe.wait_ge(lo_ready, i * 8 + u + 1)
                    pe.wait_ge(bank_free, i * 8 + u + 1)
                    product(2 + u % 2, u % 4, [[hs[b][:, k] for k in range(KD)] for b in range(2)],
                            True, True).then_inc(ff_done, 1)
            pe.wait_ge(a_ready, FT + 2)
            with pe.Fori(0, 4) as i:
                for u in range(8):
                    m = u // 4
                    pe.wait_ge(lo_ready, i * 8 + u + 33)
                    if u % 4 == 0:
                        pe.wait_ge(y_added, i * 2 + m + 1)
                    k0 = u % 4 * KD
                    product(4 + m, u % 4, [[as_[b][:, k0 + k] for k in range(KD)] for b in range(2)],
                            u % 4 == 0, u % 4 == 3).then_inc(ff_done, 1)
                    if u in (4, 7):
                        mt = 0 if u == 4 else 1
                        pe.wait_ge(y_added, i * 2 + mt + 3)
                        for t, n in ((0, P), (1, P), (2, NS)):
                            ins = pe.transpose(ps[0:n, 6 + mt, t * P:(t + 1) * P], yT[:, mt, t * P:t * P + n], ident)
                        ins.then_inc(y_turned, 1)

        @block.scalar
        def _(sc):
            sc.dma_start(const[:, 0:NFIRST], A["const"][:, 0:NFIRST]).then_inc(first_in, 16)
            sc.dma_start(ptab[:, :], A["page_rows"]).then_inc(small_in, 16)
            sc.dma_start(param[:, :], A["param"]).then_inc(small_in, 16)
            sc.dma_start(const[:, NFIRST:], A["const"][:, NFIRST:]).then_inc(const_in, 16)
            sc.dma_start(tab[0:BUCKETS, :], A["rel_bias"]).then_inc(hot_in, 16)
            sc.dma_start(tab[BUCKETS:BUCKETS + 4, :], A["group"]).then_inc(hot_in, 16)
            sc.dma_start(hot[:, :], A["hot"]).then_inc(hot_in, 16)
            for k, t in enumerate((2, 0, 1)):
                n = NS if t == 2 else P
                sc.wait_ge(x_in[t], 16)
                sc.activation(xs[0:n, t], xnat[0:n, t], ACT.Square, accum_out=ssx[0:n, t:t + 1]).then_inc(x_squared, 1)
                sc.wait_ge(x_squared, k + 1)
                if k == 0:
                    sc.wait_ge(first_in, 16)
                sc.activation(ssx[0:n, 3 + t:4 + t], ssx[0:n, t:t + 1], ACT.Sqrt, bias=cst("eps", n), scale=1.0 / D
                              ).then_inc(x_std, 1)
            sc.wait_ge(h_turned, KD)
            sc.dma_start(scv[:, :, :], A["state_conv"].rearrange("l n t c -> (l n t) c").rearrange(
                "(s q) c -> q s c", s=2)).then_inc(state_in, 16)
            sc.wait_ge(small_in, 32)
            sc.wait_ge(const_in, 16)

            def tables_out():
                sc.wait_ge(bias_made, 1)
                sc.copy(trow[:, :], ps[0:16, 2, 0:TW]).then_inc(rows_made, 1)
                sc.wait_ge(bias_made, 2)
                sc.copy(bias[:, :], ps[:, 3, 0:92]).then_inc(bias_copied, 2)

            def x_out(i):
                sc.wait_ge(x_turned, i + 1)
                sc.copy(xT[:, i], ps[:, 2 + i % 2, 0:T]).then_inc(x_copied, 1)

            def take(j):
                sc.wait_ge(z_done, j + 1)
                z = ps[:, j % 2, 0:T]
                if j in QK:
                    q = QK.index(j)
                    if q >= 2:
                        sc.wait_ge(ms_done, q - 1)
                if j in Q_UNITS:
                    zr = reversed_tiles(z[:, 0:SEQ])
                    sc.activation(sqq[:, q % 2, 0:SEQ].rearrange("p (t c) -> p t c", c=P), zr, ACT.Square).then_inc(act, 1)
                    sc.activation(sqq[:, q % 2, SEQ:T], z[:, SEQ:T], ACT.Square).then_inc(sq_ready, 1)
                    sc.copy(qkv[:, j, 0:SEQ].rearrange("p (t c) -> p t c", c=P), zr).then_inc(act, 1)
                    sc.copy(qkv[:, j, SEQ:T], z[:, SEQ:T]).then_inc(z_evac, 1)
                    return
                if j in QK:
                    sc.activation(sqq[:, q % 2], z, ACT.Square).then_inc(sq_ready, 1)
                if j < 15:
                    sc.copy(qkv[:, j], z).then_inc(z_evac, 1)
                elif j < U_A:
                    sc.activation(cb[:, j - U_B], z, ACT.Sigmoid).then_inc(z_evac, 1)
                elif j < U_G:
                    sc.copy(ca[:, j - U_A], z).then_inc(z_evac, 1)
                else:
                    sc.activation(gates[:, j - U_G], z, ACT.Identity, bias=par("b_gate", j - U_G)).then_inc(z_evac, 1)

            def deviation(q):
                sc.wait_ge(ms_done, q + 1)
                if q >= 4:
                    sc.wait_ge(qn_done, q - 3)
                sc.activation(stdq[:, q % 4], ps[:, 6 + q % 2, 0:T], ACT.Sqrt, bias=cst("eps")).then_inc(std_done, 1)

            def natural_out(i):
                kind, u, col = NAT[i]
                bank = 2 + i % 2
                sc.wait_ge(nat_done, i + 1)
                if kind in "kv":
                    dst = knat if kind == "k" else vnat
                    sc.copy(dst[:, :, col:col + P], ps[:, bank, 0:256].rearrange("p (t c) -> p t c", t=2)).then_inc(act, 1)
                if kind == "u":
                    sc.copy(unat[:, col:col + P], ps[0:HALO, bank, 0:P]).then_inc(act, 1)
                if kind == "s":
                    sc.copy(usx[:, u, :, 0:HALO], ps[:, bank, 0:240].rearrange("p (n t) -> p n t", n=NS)
                            ).then_inc(nat_evac, 1)
                else:
                    off = {"q": 0, "k": 640, "v": 1280, "u": 1920}[kind] + col
                    sc.copy(snat[:, off:off + P], ps[0:NS, bank, 256:384]).then_inc(nat_evac, 1)

            def exps():
                sc.wait_ge(sub_ready, 4)
                sc.activation(sd, sd, ACT.Exp).then_inc(exp_done, 1)
                sc.activation(sm[:, :, :], sm[:, :, :], ACT.Exp).then_inc(exp_done, 1)
                sc.activation(ln[:, :], ln[:, :], ACT.Exp).then_inc(exp_done, 1)

            def values_out(n):
                if n == 0:
                    sc.wait_ge(pvd_done, 1)
                else:
                    sc.wait_ge(pvm_done, n)
                    sc.wait_ge(vt_done, n)
                sc.copy(vo[:, :], ps[:, 7, 256:512]).then_inc(vo_ready, 1)

            def conv_square():
                sc.wait_ge(xc_ready, KC)
                sc.activation(csq[:, :, :], cb[:, :, :], ACT.Square).then_inc(csq_ready, 1)

            def conv_deviation():
                sc.wait_ge(var_done, 1)
                sc.activation(rx[:, :], ps[:, 3, 0:T], ACT.Sqrt, bias=cst("eps"), scale=1.0 / C).then_inc(cstd, 1)

            def conv_affine():
                sc.wait_ge(cy_ready, 1)
                for t in range(KC):
                    sc.activation(cact[:, t], cb[:, t], ACT.Identity, bias=par("ln_b", t), scale=par("ln_g", t)
                                  ).then_inc(cyn, 1)
                sc.wait_ge(cyn, KC)
                sc.activation(csq[:, :, :], cact[:, :, :], ACT.Sigmoid).then_inc(csg, 1)

            def prompt_exp(h):
                sc.wait_ge(l_ready, h + 1)
                for k, (lo, hi) in enumerate(((0, 384), (384, 1152), (1152, 1280), (1280, 1536))):
                    sc.activation(logits[:, lo:hi], logits[:, lo:hi], ACT.Exp, bias=nmax[:, k:k + 1],
                                  accum_out=psum_[:, k:k + 1]).then_inc(p_exp, 1)

            def probs_out(h):
                for b in range(3):
                    sc.wait_ge(pt_done, 3 * h + b + 1)
                    if h >= 1 and b == 0:
                        sc.wait_ge(o_done, h)
                    sc.copy(probT[:, b * 512:(b + 1) * 512], ps[:, 2 + b, :]).then_inc(pt_evac, 1)

            def outputs_out(h):
                sc.wait_ge(o_done, h + 1)
                r = slice(h * DH, (h + 1) * DH)
                sc.copy(oT[r, 0, 0:SEQ].rearrange("p (t c) -> p t c", c=P), reversed_tiles(ps[r, 6, 0:256])).then_inc(o_evac, 1)
                r = slice(h % 2 * ME, (h % 2 + 1) * ME)
                sc.copy(oT[r, 1 + h // 2, 0:SEQ].rearrange("p (t c) -> p t c", c=P), reversed_tiles(ps[r, 6, 256:512])).then_inc(o_evac, 1)

            for j in range(NU):
                take(j)
                if j == 1:
                    tables_out()
                if j in (2, 3):
                    for i in range(4):
                        x_out(4 * (j - 2) + i)
                if 1 <= j <= 4:
                    deviation(j - 1)
                if 7 <= j <= 12:
                    deviation(j - 3)
                for i in {4: (0, 1), 5: (2, 3), 6: (4,), 7: (5,), 11: (6,), 13: (7, 8), 16: (9, 10), 18: (11, 12),
                          19: (13,), 20: (14,), 21: (15,), 22: (16,), 23: (17,), 26: (18, 19, 20)}.get(j, ()):
                    natural_out(i)
                if j == 32:
                    exps()
                if j == 34:
                    values_out(0)
                    conv_square()
                if 37 <= j:
                    values_out(j - 36)
                if j == 35:
                    conv_deviation()
                if j == 36:
                    conv_affine()
                if j in (37, 40, 43):
                    prompt_exp((j - 37) // 3)
                if j in (38, 41, 44):
                    probs_out((j - 38) // 3)
                if j in (39, 42):
                    outputs_out((j - 39) // 3)
            outputs_out(2)
            prompt_exp(3)
            probs_out(3)
            outputs_out(3)
            gv = gates[:, :, :].rearrange("p (b i) t -> p b i t", b=3)
            for i in range(KD):
                sc.activation(gv[:, :, i], gv[:, :, i], ACT.Sigmoid).then_inc(gate_ready, 1)

            def high_ff1(i, u):
                s, n = (u // 2) % 4, u // 8
                sc.wait_ge(fw_in[s], i * 16 + 16 * (n + 1))
                sc.wait_ge(ff_done, i * 8 + u + 1)
                sc.copy(ws[0][u % 4][:, :, :], weights1(s, u % 2)).then_inc(hi_ready, 1)

            def high_ff2(i, u):
                s, n = (u // 2) % 4, u // 8
                sc.wait_ge(fw_in[s], i * 16 + 16 * (n + 5))
                sc.wait_ge(ff_done, i * 8 + u + 33)
                sc.copy(ws[0][u % 4][:, :, :], weights2(s, u % 2)).then_inc(hi_ready, 1)

            sc.wait_ge(m_ready, KD)
            for i in range(KD):
                sc.wait_ge(x1_ready, i + 1)
                sc.activation(hs[0][:, i], xT[:, i], ACT.Copy, scale=par("g_ffn", i)).then_inc(h_hi, 1)
                if i >= 2:
                    sc.wait_ge(x1_summed, i - 1)
                sc.activation(sqx[:, i % 2], xT[:, i], ACT.Square).then_inc(x1_squared, 1)
                if i >= 5 and i < 7:
                    high_ff1(0, i - 5)
            sc.wait_ge(x1_summed, KD)
            sc.activation(rx[:, :], ps[:, 0, 0:T], ACT.Sqrt, bias=cst("eps"), scale=1.0 / D).then_inc(x1_std, 1)

            def hidden(i, u):
                sc.wait_ge(bank_free, i * 8 + u + 3)
                sc.wait_ge(a_ready, i * 8 + u + 1)
                sc.activation(ra[:, u % 2], rl[:, u % 2], ACT.Square).then_inc(ra_ready, 1)

            with sc.Fori(0, 3) as i:
                for u in range(8):
                    high_ff1(i, u + 2)
                    hidden(i, u)
            for u in range(8):
                if u < 6:
                    high_ff1(3, u + 2)
                else:
                    high_ff2(0, u - 6)
                hidden(3, u)

            def rows_back(i, m):
                sc.wait_ge(y_turned, i * 2 + m + 1)
                sc.copy(ynat[:, bass.ds(i * 6 + m * 3, 2), :], ps[:, 6 + m, 0:256].rearrange("p (t c) -> p t c", t=2)
                        ).then_inc(act, 1)
                sc.copy(ynat[0:NS, bass.ds(i * 6 + m * 3 + 2, 1), :], ps[0:NS, 6 + m:7 + m, 256:384]).then_inc(y_evac, 1)

            with sc.Fori(0, 3) as i:
                for u in range(8):
                    high_ff2(i, u + 2)
                    if u in (5, 7):
                        rows_back(i, (u - 5) // 2)
            for u in range(6):
                high_ff2(3, u + 2)
                if u == 5:
                    rows_back(3, 0)
            rows_back(3, 1)

        @block.vector
        def _(v):
            steps = [0]

            def step(ins):
                steps[0] += 1
                ins.then_inc(dve, 1)
                v.wait_ge(dve, steps[0])

            v.wait_ge(small_in, 32)
            v.wait_ge(first_in, 16)
            v.tensor_scalar(pidx[:, :], ptab[:, :], float(PAGE // ROWS), cst("sub8"), ALU.mult, ALU.add
                            ).then_inc(idx_ready, 1)
            for k, t in enumerate((2, 0, 1)):
                n = NS if t == 2 else P
                v.wait_ge(x_std, k + 1)
                step(v.reciprocal(ssx[0:n, t:t + 1], ssx[0:n, 3 + t:4 + t]))
                v.tensor_scalar(xs[0:n, t], xnat[0:n, t], ssx[0:n, t:t + 1], None, ALU.mult).then_inc(x_scaled, 1)
            for i in range(KD):
                v.wait_ge(h_turned, i + 1)
                v.tensor_scalar(actT[:, i], ps[:, 4 + i % 4, 0:T], par("g_mix", i), None, ALU.mult).then_inc(h_ready, 1)
            v.wait_ge(const_in, 16)

            def norm_heads(q):
                u = QK[q]
                g = par("mqn" if q < 2 else "mkn" if q < 4 else "dqn" if q < 7 else "dkn")
                v.wait_ge(std_done, q + 1)
                v.wait_ge(z_evac, u + 1)
                if q:
                    v.wait_ge(qn_done, q)
                step(v.reciprocal(rq[:, :], stdq[:, q % 4]))
                v.scalar_tensor_tensor(qkv[:, u], qkv[:, u], g, rq[:, :], ALU.mult, ALU.mult).then_inc(qn_done, 1)

            def score_cache(n):
                k = kv[n % 2][:, :].rearrange("p (r c) -> p r c", c=MW)
                v.wait_ge(kv_in[n % 2], kv_arrived[n])
                v.wait_ge(qb_done, n + 1)
                q = ps[:, 4 + n % 2:5 + n % 2, 0:MW].broadcast_to([P, ROWS, MW])
                v.tensor_tensor(k, k, q, ALU.mult).then_inc(prod_done, 1)
                v.wait_ge(prod_done, n + 1)
                v.tensor_reduce(sm[:, n], kv[n % 2][:, :].rearrange("p (a e) -> p a e", e=ME), AX.X, ALU.add
                                ).then_inc(kred_done, 1)

            def score_state():
                v.wait_ge(kv_in[IT_SK % 2], kv_arrived[IT_SK])
                for n in range(NS):
                    v.wait_ge(qb_done, NS + n + 1)
                    v.tensor_tensor(stk[:, :, n], stk[:, :, n],
                                    ps[:, 4 + n % 2, 0:384].rearrange("p (g c) -> p g c", g=NG), ALU.mult
                                    ).then_inc(prod_done, 1)
                v.wait_ge(prod_done, 2 * NS)
                v.tensor_reduce(sd, stk[:, :, :, :].rearrange("p g n (h e) -> p (g n h) e", e=DH), AX.X, ALU.add
                                ).then_inc(kred_done, 1)

            def gate_conv():
                v.wait_ge(z_evac, U_G)
                v.tensor_tensor(uext[:, :, HALO:], ca[:, :, 0:SEQ], cb[:, :, 0:SEQ], ALU.mult).then_inc(u_ready, 1)
                v.tensor_tensor(usx[:, :, :, HALO], ca[:, :, SEQ:T], cb[:, :, SEQ:T], ALU.mult).then_inc(u_ready, 1)

            def taps(lo, hi):
                w = param[:, POFF["conv_w"][0]:POFF["conv_w"][1]].rearrange("p (c k) -> p c k", c=KC)
                for k in range(lo, hi):
                    for c in range(KC):
                        src, acc = uext[:, c, k:k + SEQ], ca[:, c, 0:SEQ]
                        if k == 0:
                            v.wait_ge(u_ready, 2)
                            v.wait_ge(padded, 1)
                            v.tensor_scalar(acc, src, w[:, c, 0:1], par("conv_b", c), ALU.mult, ALU.add
                                            ).then_inc(conv_step, 1)
                        else:
                            v.wait_ge(conv_step, KC * (k - 1) + c + 1)
                            v.scalar_tensor_tensor(acc, src, w[:, c, k:k + 1], acc, ALU.mult, ALU.add
                                                   ).then_inc(conv_step, 1)

            def sample_taps():
                v.wait_ge(nat_evac, N_U)
                v.wait_ge(u_ready, 2)
                w = param[:, POFF["conv_w"][0]:POFF["conv_w"][1]].rearrange("p (c k) -> p c k", c=KC)
                for c in range(KC):
                    step(v.tensor_tensor(usx[:, c], usx[:, c], w[:, c:c + 1, :].broadcast_to([P, NS, TAPS]), ALU.mult))
                step(v.tensor_reduce(ca[:, :, SEQ:T], usx[:, :, :, :], AX.X, ALU.add))
                b = param[:, POFF["conv_b"][0]:POFF["conv_b"][1]].unsqueeze(2).broadcast_to([P, KC, NS])
                v.wait_ge(conv_step, KC * TAPS)
                v.tensor_tensor(ca[:, :, SEQ:T], ca[:, :, SEQ:T], b, ALU.add).then_inc(conv_done, 1)

            def nh(ap):
                return ap.rearrange("p (n h) -> p n h", h=4)

            def new_products():
                v.wait_ge(z_evac, U_B)
                v.wait_ge(qn_done, len(QK))
                step(v.tensor_tensor(pnd[:, :, :], qkv[:, U_DQ:U_DQ + 3, SEQ:T], qkv[:, U_DK:U_DK + 3, SEQ:T], ALU.mult))
                step(v.tensor_tensor(pnm[:, :, :], qkv[:, U_MQ:U_MQ + 2, SEQ:T], qkv[:, U_MK:U_MK + 2, SEQ:T], ALU.mult))
                a = pnd[:, :, :].rearrange("p g n -> p (g n)").unsqueeze(2).broadcast_to([P, NG * NS, HPG])
                b = cst("hmask").unsqueeze(1).broadcast_to([P, NG * NS, HPG])
                v.tensor_tensor(rnd[:, :, :], a, b, ALU.mult).then_inc(new_ready, 1)
                a = pnm[:, :, :].unsqueeze(3).broadcast_to([P, 2, NS, MH])
                b = cst("mmask").rearrange("p (t h) -> p t h", t=2).unsqueeze(2).broadcast_to([P, 2, NS, MH])
                v.tensor_tensor(rnm[:, :, :, :], a, b, ALU.mult).then_inc(new_ready, 1)

            def rows_n(lo, width):
                return bias[:, lo:lo + width].unsqueeze(1).broadcast_to([P, NS, width])

            def sample_logits():
                v.wait_ge(new_dot, 1)
                v.wait_ge(bias_copied, 2)
                for g in range(4):
                    cols = slice(g * 32, g * 32 + 32)
                    v.scalar_tensor_tensor(nh(ln[:, cols]), nh(ps[:, 7, cols]), s_d if g < NG else s_m,
                                           rows_n(76 + 4 * g, 4), ALU.mult, ALU.add).then_inc(new_read, 1)
                v.wait_ge(kred_done, NS + 1)
                v.tensor_reduce(rt[:, :].rearrange("p (n h) -> p n h", h=MH),
                                sm[:, :, :].rearrange("p n (r h) -> p n h r", h=MH), AX.X, ALU.add).then_inc(route_ready, 1)
                for g in range(NG):
                    cols = slice(g * 32, g * 32 + 32)
                    ins = v.scalar_tensor_tensor(nh(sd[:, cols]), nh(sd[:, cols]), s_d, rows_n(64 + 4 * g, 4),
                                                 ALU.mult, ALU.add)
                step(ins)
                step(v.scalar_tensor_tensor(sm[:, :, :], sm[:, :, :], s_m, rows_n(0, 64), ALU.mult, ALU.add))

            def select_blocks():
                v.wait_ge(route_dot, 1)
                step(v.tensor_copy(r32[:, :], ps[0:32, 7, 128:136]))
                step(v.max(top[:, :], r32[:, :]))
                step(v.max_index(topi[:, :], top[:, :], r32[:, :]))
                step(v.tensor_copy(topf[:, :], topi[:, :]))
                io = cst("iota", 32)
                step(v.tensor_scalar(selb[:, :], io, topf[:, 0:1], None, ALU.is_equal))
                for k in range(1, TOPK):
                    step(v.scalar_tensor_tensor(selb[:, :], io, topf[:, k:k + 1], selb[:, :], ALU.is_equal, ALU.add))
                v.tensor_scalar(selb[:, :], selb[:, :], -NEG, NEG, ALU.mult, ALU.add).then_inc(sel_ready, 1)

            def selection_row():
                v.wait_ge(sel_turned, 1)
                v.tensor_copy(selT[:, :], ps[0:NB, 7, 136:168]).then_inc(selT_ready, 1)

            def sample_maxima():
                v.wait_ge(sel_spread, 1)
                mask = nh(ps[:, 7, 168:200]).unsqueeze(2).broadcast_to([P, NS, ROWS, MH])
                m4 = sm[:, :, :].rearrange("p n (r h) -> p n r h", h=MH)
                v.tensor_tensor(m4, m4, mask, ALU.add).then_inc(sel_read, 1)
                v.wait_ge(sel_read, 1)
                v.tensor_reduce(mc[:, 0:32], sd.rearrange("p (g m) -> p m g", g=NG), AX.X, ALU.max
                                ).then_inc(mc_ready, 1)
                v.tensor_reduce(nh(mc[:, 32:64]), sm[:, :, :].rearrange("p n (r h) -> p n h r", h=MH), AX.X, ALU.max
                                ).then_inc(mc_ready, 1)
                step(v.tensor_reduce(lmax[:, :], ln[:, 0:96].rearrange("p (g m) -> p m g", g=NG), AX.X, ALU.max))

            def spread_maxima():
                v.wait_ge(mc_turned, 1)
                step(v.tensor_reduce(mm[:, :], ps[0:64, 7, 200:328], AX.X, ALU.max))
                v.tensor_scalar(dg[:, :], ident[0:64, 0:64], mm[:, :], None, ALU.mult).then_inc(dg_ready, 1)

            def subtract_maxima():
                v.wait_ge(max_spread, 1)
                step(v.tensor_tensor(gmx[:, 0:32], ps[:, 7, 328:360], lmax[:, :], ALU.max))
                step(v.tensor_tensor(gmx[:, 32:64], ps[:, 7, 360:392], ln[:, 96:128], ALU.max))
                gd = gmx[:, 0:32].unsqueeze(1).broadcast_to([P, NG, 32])
                v3 = sd.rearrange("p (g m) -> p g m", g=NG)
                v.tensor_tensor(v3, v3, gd, ALU.subtract).then_inc(sub_ready, 1)
                m4 = sm[:, :, :].rearrange("p n (r h) -> p n r h", h=MH)
                gm = nh(gmx[:, 32:64]).unsqueeze(2).broadcast_to([P, NS, ROWS, MH])
                v.tensor_tensor(m4, m4, gm, ALU.subtract).then_inc(sub_ready, 1)
                v3 = ln[:, 0:96].rearrange("p (g m) -> p g m", g=NG)
                v.tensor_tensor(v3, v3, gd, ALU.subtract).then_inc(sub_ready, 1)
                v.tensor_tensor(ln[:, 96:128], ln[:, 96:128], gmx[:, 32:64], ALU.subtract).then_inc(sub_ready, 1)

            def sample_sums():
                v.wait_ge(exp_done, 3)
                v.tensor_reduce(ssum[:, 0:32], sd.rearrange("p (g m) -> p m g", g=NG), AX.X, ALU.add
                                ).then_inc(sum_ready, 1)
                v.tensor_reduce(nh(ssum[:, 32:64]), sm[:, :, :].rearrange("p n (r h) -> p n h r", h=MH), AX.X, ALU.add
                                ).then_inc(sum_ready, 1)
                step(v.tensor_reduce(lmax[:, :], ln[:, 0:96].rearrange("p (g m) -> p m g", g=NG), AX.X, ALU.add))

            def sample_denominators():
                v.wait_ge(den_dot, 1)
                v.tensor_tensor(gmx[:, 0:32], ps[:, 7, 392:424], lmax[:, :], ALU.add)
                v.tensor_tensor(gmx[:, 32:64], ps[:, 7, 424:456], ln[:, 96:128], ALU.add).then_inc(den_read, 1)
                v.wait_ge(den_read, 1)
                step(v.reciprocal(rden[:, :], gmx[:, :]))

            def sample_outputs():
                v.wait_ge(vt_done, NS + 1)
                vd = qkv[:, U_DV:U_DV + 3, SEQ:T].unsqueeze(3).broadcast_to([P, NG, NS, HPG])
                t1v = t1[:, :, :].rearrange("p g (n h) -> p g n h", h=HPG)
                step(v.tensor_tensor(t1v, ln[:, 0:96].rearrange("p (g n h) -> p g n h", g=NG, h=HPG), vd, ALU.mult))
                step(v.tensor_reduce(lmax[:, :], t1[:, :, :].rearrange("p g m -> p m g"), AX.X, ALU.add))
                step(v.tensor_tensor(lmax[:, :], lmax[:, :], ps[:, 7, 64:96], ALU.add))
                step(v.tensor_tensor(lmax[:, :], lmax[:, :], rden[:, 0:32], ALU.mult))
                step(v.tensor_tensor(nh(lmax[:, :]), nh(lmax[:, :]), cst("hmask").unsqueeze(1).broadcast_to([P, NS, HPG]),
                                     ALU.mult))
                v.tensor_reduce(oT[:, 0, SEQ:T], nh(lmax[:, :]), AX.X, ALU.add).then_inc(so_ready, 1)
                vm = qkv[:, U_MV:U_MV + 2, SEQ:T].unsqueeze(3).broadcast_to([P, 2, NS, MH])
                t2v = t2[:, :, :].rearrange("p t (n h) -> p t n h", h=MH)
                pn = nh(ln[:, 96:128]).unsqueeze(1).broadcast_to([P, 2, NS, MH])
                step(v.tensor_tensor(t2v, pn, vm, ALU.mult))
                step(v.tensor_tensor(t2[:, :, :], t2[:, :, :], ps[:, 7, 0:64].rearrange("p (t m) -> p t m", t=2), ALU.add))
                step(v.tensor_tensor(t2[:, :, :], t2[:, :, :], rden[:, 32:64].unsqueeze(1).broadcast_to([P, 2, 32]), ALU.mult))
                mask = cst("mmask").rearrange("p (t h) -> p t h", t=2).unsqueeze(2).broadcast_to([P, 2, NS, MH])
                step(v.tensor_tensor(t2v, t2v, mask, ALU.mult))
                v.tensor_reduce(oT[:, 1:3, SEQ:T], t2v, AX.X, ALU.add).then_inc(so_ready, 1)

            def conv_center():
                v.wait_ge(mean_done, 1)
                for t in range(KC):
                    v.scalar_tensor_tensor(cb[:, t], ps[:, 2, 0:T], -1.0 / C, ca[:, t], ALU.mult, ALU.add
                                           ).then_inc(xc_ready, 1)

            def conv_scale():
                v.wait_ge(cstd, 1)
                step(v.reciprocal(rq[:, :], rx[:, :]))
                v.tensor_tensor(cb[:, :, :], cb[:, :, :], rq[:, :].unsqueeze(1).broadcast_to([P, KC, T]), ALU.mult
                                ).then_inc(cy_ready, 1)

            def conv_swish():
                v.wait_ge(csg, 1)
                v.tensor_tensor(cact[:, :, :], cact[:, :, :], csq[:, :, :], ALU.mult).then_inc(cact_ready, 1)

            def prompt_logits(h):
                v.wait_ge(score_done, h + 1)
                v.wait_ge(e_in[h % 2], 16 * (h // 2 + 1))
                if h == 0:
                    v.wait_ge(stored, 16 * 19)
                else:
                    v.wait_ge(pt_done, 3 * h)
                e = ebias[:, h % 2]
                v.scalar_tensor_tensor(logits[:, 0:384].rearrange("p (g c) -> p g c", g=NG),
                                       ps[:, 2, 0:384].rearrange("p (g c) -> p g c", g=NG), s_d, e[:, 0:3, P:256],
                                       ALU.mult, ALU.add)
                v.scalar_tensor_tensor(logits[:, 384:1152].rearrange("p (g c) -> p g c", g=NG),
                                       ps_s1[:, 0:768].rearrange("p (g c) -> p g c", g=NG), s_d, e[:, 0:3, :],
                                       ALU.mult, ALU.add)
                v.scalar_tensor_tensor(logits[:, 1152:1280], ps[:, 5, 0:P], s_m, e[:, 3, P:256], ALU.mult, ALU.add)
                step(v.scalar_tensor_tensor(logits[:, 1280:1536], ps[:, 5, P:384], s_m, e[:, 3, :], ALU.mult, ALU.add))
                for k, (lo, hi) in enumerate(((0, 384), (384, 1152), (1152, 1280), (1280, 1536))):
                    ins = v.tensor_reduce(nmax[:, k:k + 1], logits[:, lo:hi], AX.X, ALU.max, negate=True)
                ins.then_inc(l_ready, 1)

            def prompt_probs(h):
                v.wait_ge(p_exp, 4 * (h + 1))
                step(v.reciprocal(pinv[:, :], psum_[:, :]))
                for k, (lo, hi) in enumerate(((0, 384), (384, 1152), (1152, 1280), (1280, 1536))):
                    v.tensor_scalar(logits[:, lo:hi], logits[:, lo:hi], pinv[:, k:k + 1], None, ALU.mult
                                    ).then_inc(p_ready, 1)

            for q in range(4):
                norm_heads(q)
            for n in range(NS):
                score_cache(n)
                for q in {1: (4,), 2: (5, 6), 3: (7, 8), 4: (9,)}.get(n, ()):
                    norm_heads(q)
            new_products()
            gate_conv()
            score_state()
            sample_logits()
            taps(0, 4)
            select_blocks()
            taps(4, 8)
            selection_row()
            taps(8, 12)
            sample_maxima()
            taps(12, 16)
            spread_maxima()
            taps(16, 20)
            subtract_maxima()
            taps(20, 24)
            sample_sums()
            taps(24, TAPS)
            sample_taps()
            sample_denominators()
            conv_center()
            conv_scale()
            prompt_logits(0)
            conv_swish()
            for h in range(4):
                prompt_probs(h)
                if h < 3:
                    prompt_logits(h + 1)
            sample_outputs()

            def merge(i):
                v.wait_ge(br_done, i + 1)
                v.wait_ge(gate_ready, i + 1)
                if i:
                    v.wait_ge(m_ready, i)
                b0 = 3 * (i % 2)
                g = gates[:, :, :].rearrange("p (b i) t -> p b i t", b=3)[:, :, i]
                v.tensor_tensor(mtmp[:, :, :], ps[:, b0:b0 + 3, 0:T], g, ALU.mult).then_inc(br_read, 1)
                v.wait_ge(br_read, i + 1)
                step(v.tensor_tensor(mtmp[:, 0], mtmp[:, 0], mtmp[:, 1], ALU.add))
                v.tensor_tensor(actT[:, i], mtmp[:, 0], mtmp[:, 2], ALU.add).then_inc(m_ready, 1)

            for i in range(KD):
                merge(i)

            def low_x1(k):
                v.wait_ge(h_hi, k + 1)
                v.scalar_tensor_tensor(hs[1][:, k], xT[:, k], par("g_ffn", k), hs[0][:, k].bitcast(F32),
                                       ALU.mult, ALU.subtract).then_inc(h_lo, 1)

            def low(i, u, second):
                v.wait_ge(hi_ready, i * 8 + u + 1 + (32 if second else 0))
                s = (u // 2) % 4
                v.tensor_tensor(ws[1][u % 4][:, :, :], (weights2 if second else weights1)(s, u % 2),
                                ws[0][u % 4][:, :, :].bitcast(F32), ALU.subtract).then_inc(lo_ready, 1)

            for i in range(KD):
                v.wait_ge(wo_done, i + 1)
                v.tensor_tensor(xT[:, i], xT[:, i], ps[:, 6 + i % 2, 0:T], ALU.add).then_inc(x1_ready, 1)
                if i:
                    low_x1(i - 1)
                if i >= 6:
                    low(0, i - 6, False)
            low_x1(KD - 1)
            v.sem_inc(a_ready, 2)
            v.sem_inc(y_added, 2)
            v.sem_inc(bank_free, 2)
            v.wait_ge(x1_std, 1)
            step(v.reciprocal(rinv[:, :], rx[:, :]))

            def hidden_split(i, u):
                v.wait_ge(ff_done, i * 8 + u + 5)
                v.scalar_tensor_tensor(rl[:, u % 2], ps[:, 2 + u % 2, 0:T], 0.0, rinv[:, :], ALU.max, ALU.mult
                                       ).then_inc(bank_free, 1)
                v.wait_ge(ra_ready, i * 8 + u + 1)
                t = i * 8 + u
                v.tensor_copy(as_[0][:, bass.ds(t, 1)], ra[:, u % 2:u % 2 + 1]).then_inc(ahi_ready, 1)
                v.wait_ge(ahi_ready, i * 8 + u + 1)
                v.tensor_tensor(as_[1][:, bass.ds(t, 1)], ra[:, u % 2:u % 2 + 1], as_[0][:, bass.ds(t, 1)].bitcast(F32),
                                ALU.subtract).then_inc(a_ready, 1)

            with v.Fori(0, 3) as i:
                for u in range(8):
                    low(i, u + 2, False)
                    hidden_split(i, u)
            for u in range(8):
                if u < 6:
                    low(3, u + 2, False)
                else:
                    low(0, u - 6, True)
                hidden_split(3, u)

            def add_residual(i, m):
                v.wait_ge(ff_done, i * 8 + 4 * m + 40)
                v.tensor_tensor(yT[:, m:m + 1], xT[:, bass.ds(i * 2 + m, 1)], ps[:, 4 + m:5 + m, 0:T], ALU.add
                                ).then_inc(y_added, 1)

            with v.Fori(0, 3) as i:
                for u in range(8):
                    low(i, u + 2, True)
                    if u in (3, 7):
                        add_residual(i, u // 4)
            for u in range(6):
                low(3, u + 2, True)
                if u == 3:
                    add_residual(3, 0)
            add_residual(3, 1)



_PLAIN = ['x_prompt', 'x_sample', 'state_conv', 'state_dil_k0', 'state_dil_v0', 'state_dil_k1', 'state_dil_v1',
          'state_dil_k2', 'state_dil_v2', 'cache_k', 'cache_v', 'rel_bias', 'w_in', 'w_conv_out', 'w_dil_out',
          'w_moba_out', 'w_out', 'w_ff1', 'w_ff2']
_OUTS = [("y_prompt", (1, SEQ, D)), ("y_sample", (NS, 1, D)), ("conv_p", (1, 1, HALO, C)), ("conv_s", (1, NS, HALO, C))] \
    + [(f"d{x}{g}_p", (1, 1, min(GROUPS[g][0], SEQ), HPG, DH)) for g in range(NG) for x in "kv"] \
    + [(f"d{x}{g}_s", (1, NS, GROUPS[g][0], HPG, DH)) for g in range(NG) for x in "kv"] \
    + [("k_p", (1, 1, SEQ, MH, ME)), ("v_p", (1, 1, SEQ, MH, ME)), ("k_s", (1, NS, 1, MH, ME)), ("v_s", (1, NS, 1, MH, ME))]


def kernel(**inputs):
    import concourse.bacc as _bacc
    from concourse.bass_utils import run_bass_kernel_spmd as _run

    def cols(a, k):
        return np.ascontiguousarray(np.asarray(a).reshape(k, P).T)

    a = {n: np.ascontiguousarray(inputs[n]) for n in _PLAIN}
    a["const"], a["hot"], a["group"] = shape_constants()
    a["param"] = np.concatenate(
        [cols(inputs["norm_mix_g"], KD), cols(inputs["norm_ffn_g"], KD), cols(inputs["b_gate"], 3 * KD),
         np.asarray(inputs["conv_w"])[0].reshape(TAPS, KC, P).transpose(2, 1, 0).reshape(P, KC * TAPS),
         cols(inputs["conv_b"], KC), cols(inputs["conv_ln_g"], KC), cols(inputs["conv_ln_b"], KC)]
        + [np.tile(np.asarray(inputs[n])[0], r)[:, None] for n, r in
           (("dil_qn_g", 4), ("dil_kn_g", 4), ("moba_qn_g", 2), ("moba_kn_g", 2))], axis=1)
    a["page_rows"] = np.ascontiguousarray(np.repeat(np.asarray(inputs["page_table"]).T, PAGE // ROWS, axis=0))

    nc = _bacc.Bacc("TRN2", target_bir_lowering=False, num_devices=1)
    arrays, A, O = {}, {}, {}
    for n, x in a.items():
        arrays[f"in_{n}"] = x
        A[n] = nc.dram_tensor(f"in_{n}", x.shape, mybir.dt.from_np(x.dtype), kind="ExternalInput").ap()
    for n, s in _OUTS:
        O[n] = nc.dram_tensor(f"out_{n}", s, F32, kind="ExternalOutput").ap()
    build_layer(nc, A, O)
    r = _run(nc, [arrays], core_ids=[0])
    return tuple(r.results[0][f"out_{n}"] for n, _ in _OUTS)
```

```python
from contextlib import ExitStack

import concourse.bass as bass
import numpy as np
from concourse import mybir

F32 = mybir.dt.float32
F32R = mybir.dt.float32r
I32 = mybir.dt.int32
U32 = mybir.dt.uint32
ALU = mybir.AluOpType
ACT = mybir.ActivationFunctionType
AX = mybir.AxisListType

P = 128
D = 1024
KD = D // P
SEQ, NS = 256, 8
T = SEQ + NS
C, KC, TAPS = 384, 3, 31
HALO = TAPS - 1
GROUPS = ((128, 1), (512, 4), (2048, 16))
NG, HPG, DH = 3, 4, 32
MH, ME, MW = 4, 64, 256
PAST, PAGE, BLOCK, TOPK = 2048, 128, 256, 3
NB = PAST // BLOCK
ROWS = 16
FF = 4 * D
FT = FF // P
BUCKETS, EXACT, MAXD = 32, 16, 2048
EPS = 1e-6
NEG = -1e30
TW = SEQ + P - 1

CHUNK_ORDER = [5, 6, 2, 3, 4, 1, 0] + list(range(7, 15))
UNITS = [3 * c + k for c in CHUNK_ORDER for k in range(3)]
WR = 3
U_MQ, U_MK, U_MV, U_DQ, U_DK, U_DV, U_B, U_A, U_G = 0, 2, 4, 6, 9, 12, 15, 18, 21
NU = len(UNITS)
Q_UNITS = [0, 1, 6, 7, 8]
QK = [0, 1, 2, 3, 6, 7, 8, 9, 10, 11]

OFF, _n = {}, 0
for _k, _w in (("ident", P), ("eps", 1), ("sub8", 1), ("ones", P), ("bd32", P), ("bd64", P), ("blkT", P), ("blk", NB),
               ("hmask", HPG), ("mmask", 2 * MH), ("iota", NB), ("pick4", MH), ("pick16", 4 * HPG)):
    OFF[_k] = (_n, _n + _w)
    _n += _w
NCONST = _n
NFIRST = P + 2
OH_MOBA, OH_DIL, OH_TOE = 0, ROWS // 4 * P, (ROWS // 4 + 1) * P
NHOT = OH_TOE + TW
POFF, _n = {}, 0
for _k, _w in (("g_mix", KD), ("g_ffn", KD), ("b_gate", 3 * KD), ("conv_w", KC * TAPS), ("conv_b", KC),
               ("ln_g", KC), ("ln_b", KC), ("dqn", 1), ("dkn", 1), ("mqn", 1), ("mkn", 1)):
    POFF[_k] = (_n, _n + _w)
    _n += _w
NPARAM = _n


def bucket(d):
    if d < EXACT:
        return max(int(d), 0)
    big = EXACT + int(np.log(d / EXACT) / np.log(MAXD / EXACT) * (BUCKETS - EXACT) + 1e-9)
    return min(big, BUCKETS - 1)


def shape_constants():
    c = np.zeros((P, NCONST), np.float32)
    p = np.arange(P)

    def put(name, a):
        lo, hi = OFF[name]
        c[:a.shape[0], lo:hi] = a.reshape(a.shape[0], hi - lo)

    put("ident", np.eye(P))
    put("ones", np.ones((P, P)))
    put("bd32", (p[:, None] // DH == p[None] // DH) / DH)
    put("bd64", (p[:, None] // ME == p[None] // ME) / ME)
    put("blkT", np.arange(NB)[:, None] == p[None] // (P // NB))
    put("blk", p[:, None] // (P // NB) == np.arange(NB)[None])
    put("hmask", p[:, None] // DH == np.arange(HPG)[None])
    put("mmask", np.stack([p[:, None] // ME + 2 * t == np.arange(MH)[None] for t in range(2)], 1))
    put("sub8", (p % NS)[:, None])
    put("pick4", p[:, None] % DH == np.arange(MH)[None])
    put("pick16", DH * (np.arange(16) // HPG)[None] + np.arange(16)[None] % HPG == p[:, None])
    put("iota", np.tile(np.arange(NB), (P, 1)))
    put("eps", np.full((P, 1), EPS))
    hot = np.zeros((P, NHOT), np.float32)
    for m in range(TW):
        d = 255 - m
        hot[bucket(d), OH_TOE + m] = 1.0
        for g, (w, dil) in enumerate(GROUPS):
            if d < 0 or d % dil or d > w:
                hot[BUCKETS + g, OH_TOE + m] = NEG
        if d < 0:
            hot[BUCKETS + 3, OH_TOE + m] = NEG
    for r in range(ROWS):
        for q in range(P):
            hot[r % 4 * BUCKETS + bucket(PAST - ROWS * q - r), OH_MOBA + r // 4 * P + q] = 1.0
    for g, (w, dil) in enumerate(GROUPS):
        for i in range(P):
            hot[g * BUCKETS + bucket((P - i) * dil), OH_DIL + i] = 1.0
    group = np.zeros((4, 16), np.float32)
    for g in range(4):
        group[g, 4 * g:4 * g + 4] = 1.0
    return c, hot, group


def build_layer(nc, A, O):
    base = -(-nc.sbuf_base // 32) * 32
    room = nc.sbuf_usable_end - base
    scratch = nc.dram_tensor("bias_rows", [16, TW], F32).ap()

    with ExitStack() as ctx:
        place = [0]

        def sb(name, shape, dt=F32, at=None):
            size = int(np.prod(shape[1:])) * 4
            off = place[0] if at is None else at
            t = nc.alloc_sbuf_tensor_at(name, shape, dt, offset=base + off)
            end = -(-(off + size) // 32) * 32
            if at is None:
                place[0] = end
            assert end <= room, (name, end, room)
            return t

        def sem(name):
            return ctx.enter_context(nc.semaphore(name))

        xT = sb("xT", [P, KD, T])
        const = sb("const", [P, NCONST])
        param = sb("param", [P, NPARAM])
        squ = sb("squ", [P, 2, T])
        rx = sb("rx", [P, T])
        raw_at = place[0]
        raw = [sb(f"raw{s}", [P, 3 * D]) for s in range(3)]
        rawlo = [sb(f"rawlo{s}", [P, 3 * D], F32R, at=raw_at + s * 3 * D * 4) for s in range(3)]
        acts_at = place[0]
        acts = [sb(f"acts{k}", [P, KD, T], F32R) for k in range(2)]
        whi = [sb(f"whi{s}", [P, KD, P], F32R) for s in range(WR)]
        second_half = place[0]
        gates_at = place[0]
        gates = sb("gates", [P, 3 * KD, T])
        xnat = sb("xnat", [P, 3, D], at=gates_at)
        hot = sb("hot", [P, NHOT], at=gates_at + 3 * D * 4)
        qkv = sb("qkv", [P, 15, T])
        uext_at = place[0]
        uext = sb("uext", [P, KC, HALO + SEQ])
        usx = sb("usx", [P, KC, NS, TAPS])
        ca = sb("ca", [P, KC, T])
        cb = sb("cb", [P, KC, T])
        csq = sb("csq", [P, KC, T], at=uext_at)
        vnat = sb("vnat", [P, 2, 640])
        ebias_at = place[0]
        ebias = sb("ebias", [P, 2, 4, 256])
        oT = sb("oT", [P, 3, T])
        qnat = sb("qnat", [NS, 640])
        snat = sb("snat", [NS, 1664], at=ebias_at + 4 * 256 * 4)
        logits_at = place[0]
        logits = sb("logits", [P, 1536])
        knat = sb("knat", [P, 2, 640], at=logits_at)
        probT_at = place[0]
        probT = sb("probT", [P, 1536])
        kv_at = place[0]
        kv = [sb(f"kv{s}", [P, ROWS * MW]) for s in range(2)]
        stk = sb("stk", [P, NG, NS, P], at=kv_at)
        stv = sb("stv", [P, NG, NS, P], at=raw_at)
        stdq = sb("stdq", [P, 4, T])
        scv = sb("scv", [NS * HALO // 2, 2, C], at=probT_at)
        unat = sb("unat", [HALO, C], at=probT_at + 2 * C * 4)
        trow = sb("trow", [16, TW], at=gates_at + 3 * D * 4 + NHOT * 4 + 4)
        tab = sb("tab", [BUCKETS + 4, 16])
        tabm = sb("tabm", [P, 4 * MH + NG * HPG])
        bias = sb("bias", [P, 92])
        ptab = sb("ptab", [P, NS], I32)
        pidx = sb("pidx", [P, NS], I32)
        smp = sb("sm", [P, NS * ROWS * MH + DH - MH])
        sm = smp[:, 0:NS * ROWS * MH].rearrange("p (n c) -> p n c", n=NS)
        sdp = sb("sd", [P, NG * 32 + DH - HPG])
        sd = sdp[:, 0:NG * 32]
        vo = sb("vo", [P, MW])
        vd_t = sb("vd_t", [P, 32])
        pnd = sb("pnd", [P, NG, NS])
        pnm = sb("pnm", [P, 2, NS])
        rnd = sb("rnd", [P, NG * NS, HPG])
        rnm = sb("rnm", [P, 2, NS, MH])
        ln = sb("ln", [P, 128])
        rt = sb("rt", [P, 32])
        r32 = sb("r32", [32, NB])
        top = sb("top", [32, 8])
        topi = sb("topi", [32, 8], U32)
        topf = sb("topf", [32, 8])
        selb = sb("selb", [32, NB])
        selT = sb("selT", [NB, 32])
        mc = sb("mc", [P, 64])
        mm = sb("mm", [64, 1])
        dg = sb("dg", [64, 64])
        lmax = sb("lmax", [P, 32])
        gmx = sb("gmx", [P, 64])
        ssum = sb("ssum", [P, 64])
        rden = sb("rden", [P, 64])
        t1 = sb("t1", [P, NG, 32])
        t2 = sb("t2", [P, 2, 32])
        nmax = sb("nmax", [P, 4])
        psum_ = sb("psum_", [P, 4])
        pinv = sb("pinv", [P, 4])
        xs = sb("xs", [P, 3, D], at=logits_at)
        ssx = sb("ssx", [P, 8])
        mtmp = sb("mtmp", [P, 2, 3, T], at=logits_at)
        place[0] = second_half
        hs = [sb(f"hs{k}", [P, KD, T], F32R) for k in range(2)]
        as_ = [sb(f"as{k}", [P, FT, T], F32R) for k in range(2)]
        ws = [[sb(f"ws{k}_{s}", [P, KD, P], F32R) for s in range(4)] for k in range(2)]
        rinv = sb("rinv", [P, T])
        rl = sb("rl", [P, 2, T])
        ra = sb("ra", [P, 2, T])
        yT = sb("yT", [P, 2, T])
        ynat = sb("ynat", [P, 3 * KD, P], at=acts_at)
        fraw = [sb(f"fraw{s}", [P, 2 * D], at=raw_at + (3 + s) % 4 * 2 * D * 4) for s in range(4)]

        ps = ctx.enter_context(nc.psum_tensor("ps", [P, 8, 512], F32))

        def cst(name, rows=P):
            return const[0:rows, OFF[name][0]:OFF[name][1]]

        def par(name, k=0):
            return param[:, POFF[name][0] + k:POFF[name][0] + k + 1]

        ident, ones = cst("ident"), cst("ones")
        ps_s1 = ps[:, 3:5, :].rearrange("p a b -> p (a b)")

        first_in, const_in, page_in, hot_in, small_in, state_in = (sem(n) for n in (
            "first_in", "const_in", "page_in", "hot_in", "small_in", "state_in"))
        unit_in = [sem(f"unit_in{u}") for u in range(3)]
        x_in = [sem(f"x_in{t}") for t in range(3)]
        w_in = [sem(f"w_in{s}") for s in range(3)]
        kv_in = [sem(f"kv_in{s}") for s in range(2)]
        e_in = [sem(f"e_in{s}") for s in range(2)]
        fw_in = [sem(f"fw_in{s}") for s in range(4)]
        rows_out, sv_in = sem("rows_out"), sem("sv_in")
        tab_clear, tab_in = sem("tab_clear"), sem("tab_in")
        stored, conv_stored, copied, y_stored = sem("stored"), sem("conv_stored"), sem("copied"), sem("y_stored")
        x_squared, x_std, x_scaled, h_turned, h_ready, x_turned, x_copied = (sem(n) for n in (
            "x_squared", "x_std", "x_scaled", "h_turned", "h_ready", "x_turned", "x_copied"))
        rows_made, bias_made, bias_copied = sem("rows_made"), sem("bias_made"), sem("bias_copied")
        idx_ready = sem("idx_ready")
        whi_ready, wlo_ready, hin_hi, m_hi = sem("whi_ready"), sem("wlo_ready"), sem("hin_hi"), sem("m_hi")
        m_sum, inv_ready = sem("m_sum"), sem("inv_ready")
        z_done, z_evac = sem("z_done"), sem("z_evac")
        sq_ready, ms_done, std_done, qn_done = sem("sq_ready"), sem("ms_done"), sem("std_done"), sem("qn_done")
        nat_done, nat_evac = sem("nat_done"), sem("nat_evac")
        qb_done, prod_done, kred_done = sem("qb_done"), sem("prod_done"), sem("kred_done")
        padded, u_ready, conv_done = sem("padded"), sem("u_ready"), sem("conv_done")
        conv_step = sem("conv_step")
        dve = sem("dve_step")
        new_ready, new_dot, new_read = sem("new_ready"), sem("new_dot"), sem("new_read")
        route_ready, route_dot, sel_ready, sel_turned, selT_ready, sel_spread, sel_read = (sem(n) for n in (
            "route_ready", "route_dot", "sel_ready", "sel_turned", "selT_ready", "sel_spread", "sel_read"))
        mc_ready, mc_turned, dg_ready, max_spread, sub_ready, exp_done, sum_ready, den_dot, den_read = (
            sem(n) for n in ("mc_ready", "mc_turned", "dg_ready", "max_spread", "sub_ready", "exp_done",
                             "sum_ready", "den_dot", "den_read"))
        pvd_done, pvm_done, so_ready = sem("pvd_done"), sem("pvm_done"), sem("so_ready")
        vo_ready, vt_done = sem("vo_ready"), sem("vt_done")
        mean_done, xc_ready, csq_ready, var_done, cstd, cy_ready, cyn, csg, cact_ready = (sem(n) for n in (
            "mean_done", "xc_ready", "csq_ready", "var_done", "cstd", "cy_ready", "cyn", "csg", "cact_ready"))
        score_done, l_ready, p_exp, p_ready, pt_done, pt_evac, o_done, o_evac = (sem(n) for n in (
            "score_done", "l_ready", "p_exp", "p_ready", "pt_done", "pt_evac", "o_done", "o_evac"))
        gate_ready, br_done, br_read, m_ready = sem("gate_ready"), sem("br_done"), sem("br_read"), sem("m_ready")
        wo_done, x1_ready, x1_squared, x1_added, x1_summed, x1_std = (sem(n) for n in (
            "wo_done", "x1_ready", "x1_squared", "x1_added", "x1_summed", "x1_std"))
        h_hi, h_lo = sem("h_hi"), sem("h_lo")
        hi_ready, lo_ready, ff_done, bank_free = (sem(n) for n in (
            "hi_ready", "lo_ready", "ff_done", "bank_free"))
        ahi_ready, ra_ready, a_ready = sem("ahi_ready"), sem("ra_ready"), sem("a_ready")
        y_added, y_turned, y_evac = sem("y_added"), sem("y_turned"), sem("y_evac")

        w_in_v = A["w_in"].rearrange("l (k p) n -> p (l k) n", p=P)
        w_co = A["w_conv_out"].rearrange("l (k p) n -> p (l k) n", p=P)
        w_do = A["w_dil_out"].rearrange("l (k p) n -> p (l k) n", p=P)
        w_mo = A["w_moba_out"].rearrange("l (k p) n -> p (l k) n", p=P)
        w_o = A["w_out"].rearrange("l (k p) n -> p (l k) n", p=P)
        w1_v = A["w_ff1"].rearrange("l (k p) n -> p (l k) n", p=P)
        w2_v = A["w_ff2"].rearrange("l (k p) n -> p (l k) n", p=P)
        NCH = 20
        BR0, BR1, WO0 = 15, 16, 17
        parts = [0] + [1] * 15 + [2] + [1] * 3
        arrived = [16 * sum(parts[k] for k in range(c % 3, c + 1, 3)) for c in range(NCH)]

        def raw3(c, tiles=raw):
            return tiles[c % 3][:, :].rearrange("p (k n) -> p k n", n=C)

        def rawb(c):
            return raw[c % 3][:, :].rearrange("p (k n) -> p k n", n=D)

        NAT = ([("q", U_MQ + t, 384 + P * t) for t in range(2)] + [("k", U_MK + t, 384 + P * t) for t in range(2)]
               + [("v", U_MV + t, 384 + P * t) for t in range(2)] + [("q", U_DQ + t, P * t) for t in range(3)]
               + [("k", U_DK + t, P * t) for t in range(3)] + [("v", U_DV + t, P * t) for t in range(3)]
               + [("s", t, 0) for t in range(3)] + [("u", t, P * t) for t in range(3)])
        N_Q, N_V, N_U = 9, 15, 21

        IT_SK, IT_V, ITEMS = NS, NS + 1, 2 * NS + 1
        kv_parts = [1] * 8 + [3] + [1] * 8
        kv_arrived = [16 * sum(kv_parts[k] for k in range(s % 2, s + 1, 2)) for s in range(ITEMS)]

        SPREAD_BANK = [4, 5, 4, 5, 4, 7, 7, 7] + [6, 7] * 4
        NAT_AT = {3: (0, 1), 10: (2, 3), 11: (4,), 12: (5,), 15: (6, 7), 16: (8,), 20: (9,), 21: (10,), 22: (11, 12),
                  23: (13, 14), 24: (15, 16), 25: (17, 18), 26: (19, 20)}
        SPREAD_AT = {4: (0, 1), 8: (2,), 12: (3,), 16: (4,), 21: (5,), 27: (6,), 31: (7,), 33: (8, 9),
                     34: (10, 11, 12, 13, 14, 15)}
        SCORES_AT, TURN_AT, VALUES_AT = [26, 32, 41], [31, 35], [32, 36]
        CHAIN = 34
        KV_AT = [8, 11, 15, 20, 24, 30, 33, 36, 39, 44, 44, 44, 44, 44, 44]
        s_d, s_m = DH ** -0.5, ME ** -0.5
        state = [(A[f"state_dil_k{g}"], A[f"state_dil_v{g}"], O[f"dk{g}_s"], O[f"dv{g}_s"]) for g in range(3)]

        def raw_unit(u, tiles=raw):
            return raw3(u // 3 if u < NU else WO0 + (u - NU) // 3, tiles)[:, :, u % 3 * P:(u % 3 + 1) * P]

        def weights1(slot, u):
            return fraw[slot][:, :].rearrange("p (k n) -> p k n", n=2 * P)[:, :, u * P:(u + 1) * P]

        def weights2(slot, u):
            return fraw[slot][:, u * D:(u + 1) * D].rearrange("p (k n) -> p k n", n=P)

        block = ctx.enter_context(nc.Block())

        def reversed_tiles(ap):
            return ap.rearrange("p (t c) -> p t c", c=P)[:, :, ::-1]

        def load_bias(eng, h):
            src = bass.AP(scratch.tensor, h * TW, [[1, P], [HPG * TW, 4], [1, 256]])
            eng.dma_start(ebias[:, h % 2], src).then_inc(e_in[h % 2], 16)

        @block.sync
        def _(sp):
            xp = A["x_prompt"].rearrange("b (t p) d -> p (b t) d", p=P)
            sp.dma_start(xnat[0:NS, 2, :], A["x_sample"].rearrange("b t d -> (b t) d")).then_inc(x_in[2], 16)
            for t in range(2):
                sp.dma_start(xnat[:, t], xp[:, t]).then_inc(x_in[t], 16)

            def load(c):
                if c >= 3:
                    last = c - 3
                    if last < 15:
                        sp.wait_ge(z_done, 3 * last + 3)
                    elif last < WO0:
                        sp.wait_ge(br_done, KD)
                    if c == BR0:
                        sp.wait_ge(pvd_done, 1)
                    if c in (BR0, WO0):
                        sp.wait_ge(pvm_done, NS - 1)
                if c == 0:
                    for u in range(3):
                        k = CHUNK_ORDER[0] * C + u * P
                        sp.dma_start(raw_unit(u), w_in_v[:, :, k:k + P]).then_inc(unit_in[u], 16)
                elif c < 15:
                    k = CHUNK_ORDER[c]
                    sp.dma_start(raw3(c), w_in_v[:, :, k * C:(k + 1) * C]).then_inc(w_in[c % 3], 16)
                elif c == BR0:
                    sp.dma_start(rawb(c), w_co).then_inc(w_in[c % 3], 16)
                elif c == BR1:
                    sp.dma_start(rawb(c)[:, 0:1, :], w_do).then_inc(w_in[c % 3], 16)
                    sp.dma_start(rawb(c)[:, 1:3, :], w_mo).then_inc(w_in[c % 3], 16)
                else:
                    k = c - WO0
                    n = min(C, D - k * C)
                    sp.dma_start(raw3(c)[:, :, 0:n], w_o[:, :, k * C:k * C + n]).then_inc(w_in[c % 3], 16)

            def copy_state(n):
                for g in (1, 2):
                    w = GROUPS[g][0]
                    for src, dst in ((state[g][0], state[g][2]), (state[g][1], state[g][3])):
                        a = src.rearrange("l n w h e -> (l n) (w h e)")[bass.ds(n, 1), P:w * P]
                        b = dst.rearrange("l n w h e -> (l n) (w h e)")[bass.ds(n, 1), 0:(w - 1) * P]
                        sp.dma_start(b, a).then_inc(copied, 16)

            for c in list(range(BR0)) + [BR1, BR0, WO0]:
                load(c)
                if c == 2:
                    sp.wait_ge(tab_clear, 1)
                    for a in range(4):
                        sp.dma_start(tabm[a * BUCKETS:(a + 1) * BUCKETS, a * MH:(a + 1) * MH],
                                     A["rel_bias"][:, NG * HPG:]).then_inc(tab_in, 16)
                    for g in range(NG):
                        sp.dma_start(tabm[g * BUCKETS:(g + 1) * BUCKETS, 4 * MH + g * HPG:4 * MH + (g + 1) * HPG],
                                     A["rel_bias"][:, g * HPG:(g + 1) * HPG]).then_inc(tab_in, 16)
                if c == 5:
                    sp.wait_ge(rows_made, 1)
                    sp.dma_start(scratch, trow[:, :]).then_inc(rows_out, 16)
                    sp.wait_ge(rows_out, 16)
                    load_bias(sp, 0)
                if c == 10:
                    sp.wait_ge(nat_evac, N_V)
                    for g, (w, _) in enumerate(GROUPS):
                        t0 = 0 if w > P else 1
                        for src, o in ((knat, O[f"dk{g}_p"]), (vnat, O[f"dv{g}_p"])):
                            sp.dma_start(o.rearrange("l b (t p) h e -> p (l b t) (h e)", p=P),
                                         src[:, t0:2, g * P:(g + 1) * P]).then_inc(stored, 16)
                        for col, o in ((0, O[f"dk{g}_s"]), (640, O[f"dv{g}_s"])):
                            r = o.rearrange("l n w h e -> (l n) w (h e)")
                            sp.dma_start(r[:, w - 1, :], snat[:, col + g * P:col + (g + 1) * P]).then_inc(stored, 16)
                    for src, o in ((knat, O["k_p"]), (vnat, O["v_p"])):
                        sp.dma_start(o.rearrange("l b (t p) h e -> p (l b t) (h e)", p=P),
                                     src[:, :, 384:640]).then_inc(stored, 16)
                    for col, o in ((0, O["k_s"]), (640, O["v_s"])):
                        sp.dma_start(o.rearrange("l n t h e -> (l n t) (h e)"),
                                     snat[:, col + 384:col + 640]).then_inc(stored, 16)
                if c == 11:
                    sp.wait_ge(nat_evac, N_U)
                    sp.dma_start(O["conv_p"].rearrange("l b t c -> (l b t) c"), unat[:, :]).then_inc(conv_stored, 16)
                    o = O["conv_s"].rearrange("l n t c -> (l n) t c")
                    sp.dma_start(o[:, HALO - 1, :], snat[:, 1280:1664]).then_inc(conv_stored, 16)
                    sp.dma_start(o[:, 0:HALO - 1, :],
                                 A["state_conv"].rearrange("l n t c -> (l n) t c")[:, 1:HALO, :]).then_inc(conv_stored, 16)
                if c in (13, 14):
                    sp.wait_ge(l_ready, c - 12)
                    load_bias(sp, c - 11)
                if c == 14:
                    sp.wait_ge(z_done, 39)
                    for g, (w, dil) in enumerate(GROUPS):
                        src = state[g][1].rearrange("l n (i d) h e -> i d (l n) (h e)", d=dil)
                        sp.dma_start(stv[:, g], src[:, 0]).then_inc(sv_in, 16)
                if c == 12:
                    sp.wait_ge(stored, 16 * 16)
                    sp.wait_ge(conv_stored, 16 * 3)
                    load_bias(sp, 1)
            copy_state(0)
            copy_state(1)
            for src, dst in ((state[0][0], state[0][2]), (state[0][1], state[0][3])):
                a = src.rearrange("l n w h e -> (l n) (w h e)")[:, P:P * P]
                b = dst.rearrange("l n w h e -> (l n) (w h e)")[:, 0:(P - 1) * P]
                sp.dma_start(b, a).then_inc(copied, 16)
            load(NCH - 2)
            load(NCH - 1)

            def load_ff(i, s, second):
                if second:
                    c = i * 4 + s
                    src = w2_v[:, (s % 2) * 16:(s % 2) * 16 + 16, bass.ds(i * 256 + (s // 2) * P, P)]
                    sp.dma_start(fraw[s][:, :].rearrange("p (k n) -> p k n", n=P), src).then_inc(fw_in[s], 16)
                else:
                    src = w1_v[:, :, bass.ds(i * 1024 + s * 256, 256)]
                    sp.dma_start(fraw[s][:, :].rearrange("p (k n) -> p k n", n=256), src).then_inc(fw_in[s], 16)

            for s in range(4):
                sp.wait_ge(wo_done, (3, 6, 8, 8)[s])
                load_ff(0, s, False)
            with sp.Fori(1, 4) as i:
                for s in range(4):
                    sp.wait_ge(lo_ready, i * 8 + 2 * s - 6)
                    load_ff(i, s, False)
                copy_state(i + 1)
            yp = O["y_prompt"].rearrange("b (t p) d -> p (b t) d", p=P)
            ys = O["y_sample"].rearrange("b t d -> (b t) d")

            def store_y(m):
                sp.wait_ge(y_evac, m + 1)
                sp.dma_start(yp[:, :, bass.ds(m * P, P)], ynat[:, bass.ds(m * 3, 2), :]).then_inc(y_stored, 16)
                sp.dma_start(ys[:, bass.ds(m * P, P)], ynat[0:NS, bass.ds(m * 3 + 2, 1), :].rearrange(
                    "p a b -> p (a b)")).then_inc(y_stored, 16)

            for s in range(4):
                sp.wait_ge(lo_ready, 32 + 2 * s - 6)
                load_ff(0, s, True)
            copy_state(5)

            def load_and_store(i, copy):
                for s in range(4):
                    sp.wait_ge(lo_ready, i * 8 + 32 + 2 * s - 6)
                    load_ff(i, s, True)
                if copy:
                    copy_state(i + 5)
                for m in range(2):
                    store_y(i * 2 + m - 2)

            with sp.Fori(1, 3) as i:
                load_and_store(i, True)
            load_and_store(3, False)
            for m in (6, 7):
                store_y(m)
            sp.wait_ge(y_stored, 16 * 2 * KD)
            sp.wait_ge(stored, 16 * 16)
            sp.wait_ge(conv_stored, 16 * 3)
            sp.wait_ge(copied, 16 * (4 * NS + 2))

        @block.gpsimd
        def _(pool):
            pool.dma_start(ptab[:, :], A["page_rows"]).then_inc(page_in, 16)
            pool.dma_start(const[:, NFIRST:], A["const"][:, NFIRST:]).then_inc(const_in, 16)
            pool.dma_start(tab[0:BUCKETS, :], A["rel_bias"]).then_inc(hot_in, 16)
            pool.dma_start(tab[BUCKETS:BUCKETS + 4, :], A["group"]).then_inc(hot_in, 16)
            pool.memset(tabm[:, :], 0.0).then_inc(tab_clear, 1)
            pool.memset(uext[:, :, 0:HALO], 0.0).then_inc(padded, 1)
            pool.memset(smp[:, NS * ROWS * MH:], 0.0).then_inc(padded, 1)
            pool.memset(sdp[:, NG * 32:], 0.0).then_inc(padded, 1)
            pool.wait_ge(idx_ready, 1)
            pages = [A[k].rearrange("l n (c r) h e -> (l n c) (r h e)", r=ROWS) for k in ("cache_k", "cache_v")]

            def load_kv(s):
                if 2 <= s <= IT_V + 1:
                    pool.wait_ge(kred_done, s - 1)
                elif s > IT_V + 1:
                    pool.wait_ge(pvm_done, s - IT_V - 1)
                if s == IT_SK:
                    for g, (w, dil) in enumerate(GROUPS):
                        src = state[g][0].rearrange("l n (i d) h e -> i d (l n) (h e)", d=dil)
                        pool.dma_start(stk[:, g], src[:, 0]).then_inc(kv_in[s % 2], 16)
                else:
                    n = s if s < IT_SK else s - IT_V
                    pool.indirect_dma_start(kv[s % 2][:, :], None, pages[s >= IT_V],
                                            bass.IndirectOffsetOnAxis(ap=pidx[:, n:n + 1], axis=0)
                                            ).then_inc(kv_in[s % 2], 16)

            def low(u):
                pool.wait_ge(whi_ready, u + 1)
                pool.tensor_tensor(raw_unit(u, rawlo), raw_unit(u), whi[u % WR][:, :, :].bitcast(F32), ALU.subtract
                                   ).then_inc(wlo_ready, 1)

            load_kv(0)
            pool.dma_start(hot[:, :], A["hot"]).then_inc(hot_in, 16)
            load_kv(1)
            for u in range(NU + KD):
                low(u)
                for s, at in enumerate(KV_AT):
                    if at == u:
                        load_kv(s + 2)

        @block.tensor
        def _(pe):
            def turn_h():
                pe.wait_ge(first_in, 16)
                pe.wait_ge(x_scaled, 3)
                for i in range(KD):
                    if i >= 4:
                        pe.wait_ge(h_ready, i - 3)
                    for t, n in ((0, P), (1, P), (2, NS)):
                        ins = pe.transpose(ps[:, 4 + i % 4, t * P:t * P + n], xs[0:n, t, i * P:(i + 1) * P],
                                           ident[0:n, 0:n])
                    ins.then_inc(h_turned, 1)

            def turn_x(i):
                if i >= 2:
                    pe.wait_ge(x_copied, i - 1)
                bank = 2 + i % 2
                if i < 2:
                    pe.wait_ge(bias_copied, 2)
                for t, n in ((0, P), (1, P), (2, NS)):
                    ins = pe.transpose(ps[:, bank, t * P:t * P + n], xnat[0:n, t, i * P:(i + 1) * P], ident[0:n, 0:n])
                ins.then_inc(x_turned, 1)

            def bias_tables():
                pe.wait_ge(const_in, 16)
                pe.wait_ge(hot_in, 48)
                pe.wait_ge(nat_evac, 2)
                pe.matmul(ps[0:16, 2, 0:TW], tab[:, :], hot[0:BUCKETS + 4, OH_TOE:OH_TOE + TW],
                          start=True, stop=True).then_inc(bias_made, 1)
                pe.wait_ge(tab_in, 16 * (4 + NG))
                for m in range(ROWS // 4):
                    pe.matmul(ps[:, 3, m * 16:(m + 1) * 16], hot[:, OH_MOBA + m * P:OH_MOBA + (m + 1) * P],
                              tabm[:, 0:4 * MH], start=True, stop=True)
                pe.matmul(ps[:, 3, 64:64 + NG * HPG], hot[0:NG * BUCKETS, OH_DIL:OH_DIL + P],
                          tabm[0:NG * BUCKETS, 4 * MH:], start=True, stop=True)
                pe.matmul(ps[:, 3, 76:92], ones[0:1, :], tab[0:1, :], start=True, stop=True).then_inc(bias_made, 1)

            def exact(out, u, k):
                hi, lo = whi[u % WR][:, k], raw_unit(u, rawlo)[:, k]
                pe.matmul(out, hi, acts[0][:, k], start=k == 0, stop=False)
                pe.matmul(out, hi, acts[1][:, k], start=False, stop=False)
                return pe.matmul(out, lo, acts[0][:, k], start=False, stop=k == KD - 1)

            def unit(j):
                pe.wait_ge(wlo_ready, j + 1)
                if j >= 2:
                    pe.wait_ge(z_evac, j - 1)
                for k in range(KD):
                    if j == 0:
                        pe.wait_ge(h_ready, k + 1)
                    ins = exact(ps[:, j % 2, 0:T], j, k)
                ins.then_inc(z_done, 1)

            def mean_square(q):
                pe.wait_ge(const_in, 16)
                pe.wait_ge(sq_ready, q + 1)
                if q >= 2:
                    pe.wait_ge(std_done, q - 1)
                bd = cst("bd64") if q < 4 else cst("bd32")
                pe.matmul(ps[:, 6 + q % 2, 0:T], bd, squ[:, q % 2], start=True, stop=True).then_inc(ms_done, 1)

            def natural(i):
                kind, u, _ = NAT[i]
                bank = 2 + i % 2
                if i in (2, 3):
                    pe.wait_ge(x_copied, KD)
                elif i > 3:
                    pe.wait_ge(nat_evac, i - 1)
                if kind in "qk":
                    pe.wait_ge(qn_done, QK.index(u) + 1)
                elif kind == "v":
                    pe.wait_ge(z_evac, u + 1)
                if kind in "kv":
                    for t in range(2):
                        pe.transpose(ps[:, bank, t * P:(t + 1) * P], qkv[:, u, t * P:(t + 1) * P], ident)
                if kind in "qkv":
                    ins = pe.transpose(ps[0:NS, bank, 256:384], qkv[:, u, SEQ:T], ident)
                elif kind == "s":
                    pe.wait_ge(state_in, 16)
                    for t in range(2):
                        ins = pe.transpose(ps[:, bank, t * 120:(t + 1) * 120], scv[:, t, u * P:(u + 1) * P],
                                           ident[0:120, 0:120])
                else:
                    pe.wait_ge(u_ready, 2)
                    pe.transpose(ps[0:HALO, bank, 0:P], uext[:, u, SEQ:SEQ + HALO], ident)
                    ins = pe.transpose(ps[0:NS, bank, 256:384], usx[:, u, :, HALO], ident)
                ins.then_inc(nat_done, 1)

            def spread_query(n):
                pe.wait_ge(nat_evac, 2 if n < NS else N_Q)
                if n == NS:
                    pe.wait_ge(o_evac, 2)
                elif n in (6, 7):
                    pe.wait_ge(prod_done, n)
                elif n >= 2:
                    pe.wait_ge(prod_done, n - 1)
                lo, hi = (384, 640) if n < NS else (0, 384)
                sel = ident[0:NS, n % NS:n % NS + 1].broadcast_to([NS, P])
                pe.matmul(ps[:, SPREAD_BANK[n], 0:hi - lo], sel, qnat[:, lo:hi], start=True, stop=True).then_inc(qb_done, 1)

            def new_logits():
                pe.wait_ge(new_ready, 2)
                pe.wait_ge(prod_done, 2 * NS)
                pe.matmul(ps[:, 7, 0:96], ones, rnd[:, :, :].rearrange("p a b -> p (a b)"), start=True, stop=True)
                for t in range(2):
                    ins = pe.matmul(ps[:, 7, 96:128], ones, rnm[:, t].rearrange("p a b -> p (a b)"),
                                    start=t == 0, stop=t == 1)
                ins.then_inc(new_dot, 1)

            def route():
                pe.wait_ge(route_ready, 1)
                pe.wait_ge(new_read, 4)
                pe.matmul(ps[0:32, 7, 128:136], rt[:, :], cst("blk"), start=True, stop=True).then_inc(route_dot, 1)

            def turn_selection():
                pe.wait_ge(sel_ready, 1)
                pe.transpose(ps[0:NB, 7, 136:168], selb[:, :], ident[0:32, 0:32]).then_inc(sel_turned, 1)

            def spread_selection():
                pe.wait_ge(selT_ready, 1)
                pe.matmul(ps[:, 7, 168:200], cst("blkT", NB), selT[:, :], start=True, stop=True).then_inc(sel_spread, 1)

            def turn_max():
                pe.wait_ge(sel_read, 1)
                pe.wait_ge(mc_ready, 2)
                pe.transpose(ps[0:64, 7, 200:328], mc[:, :], ident).then_inc(mc_turned, 1)

            def spread_max():
                pe.wait_ge(dg_ready, 1)
                pe.matmul(ps[:, 7, 328:392], ones[0:64, :], dg[:, :], start=True, stop=True).then_inc(max_spread, 1)

            def denominators():
                pe.wait_ge(sum_ready, 2)
                pe.wait_ge(vo_ready, 1)
                pe.matmul(ps[:, 7, 128:192], ones, ssum[:, :], start=True, stop=True).then_inc(den_dot, 1)

            def values_dilated():
                pe.wait_ge(exp_done, 3)
                pe.wait_ge(padded, 3)
                pe.wait_ge(sv_in, 16 * NG)
                for half in range(2):
                    for g in range(NG):
                        for j in range(4):
                            n = 4 * half + j
                            ins = pe.matmul(ps[j * DH:(j + 1) * DH, 7, 256 + half * P:256 + (half + 1) * P],
                                            sdp[:, g * 32 + 4 * n:g * 32 + 4 * n + DH], stv[:, g, n],
                                            start=g == 0, stop=g == NG - 1, tile_position=(0, j * DH))
                ins.then_inc(pvd_done, 1)

            def turn_dilated():
                pe.wait_ge(den_read, 1)
                for half in range(2):
                    ins = pe.matmul(ps[:, 7, 64 + 16 * half:80 + 16 * half], vo[:, half * P:(half + 1) * P], cst("pick16"),
                                    start=True, stop=True)
                ins.then_inc(vt_done, 1)

            def values_moba(n):
                it = IT_V + n
                pe.wait_ge(kv_in[it % 2], kv_arrived[it])
                pe.wait_ge(vo_ready, n + 1)
                vv = kv[it % 2][:, :].rearrange("p (r c) -> p r c", c=MW)
                for r in range(ROWS):
                    j = r % 4
                    ins = pe.matmul(ps[j * DH:(j + 1) * DH, 7, 256:512],
                                    smp[:, n * ROWS * MH + MH * r:n * ROWS * MH + MH * r + DH], vv[:, r],
                                    start=r < 4, stop=r >= ROWS - 4, tile_position=(0, j * DH))
                ins.then_inc(pvm_done, 1)

            def turn_moba(n):
                pe.wait_ge(vo_ready, n + 2)
                for t in range(2):
                    ins = pe.matmul(ps[:, 7, t * 32 + 4 * n:t * 32 + 4 * n + 4], vo[:, t * P:(t + 1) * P], cst("pick4"),
                                    start=True, stop=True)
                ins.then_inc(vt_done, 1)

            def conv_mean():
                pe.wait_ge(conv_done, 1)
                pe.wait_ge(z_evac, NU)
                for t in range(KC):
                    ins = pe.matmul(ps[:, 0, 0:T], ones, ca[:, t], start=t == 0, stop=t == KC - 1)
                ins.then_inc(mean_done, 1)

            def conv_var():
                pe.wait_ge(csq_ready, 1)
                for t in range(KC):
                    ins = pe.matmul(ps[:, 1, 0:T], ones, csq[:, t], start=t == 0, stop=t == KC - 1)
                ins.then_inc(var_done, 1)

            def scores(h):
                if h == 0:
                    pe.wait_ge(prod_done, 5)
                    pe.wait_ge(nat_evac, N_U)
                else:
                    pe.wait_ge(pt_evac, 3 * h)
                r = slice(h * DH, (h + 1) * DH)
                for g in range(NG):
                    pe.matmul(ps[:, 2, g * P:(g + 1) * P], qkv[r, U_DQ + g, 0:P], qkv[r, U_DK + g, 0:P],
                              start=True, stop=True)
                for g in range(NG):
                    pe.matmul(ps_s1[:, g * 256:(g + 1) * 256], qkv[r, U_DQ + g, P:SEQ], qkv[r, U_DK + g, 0:SEQ],
                              start=True, stop=True)
                r = slice(h % 2 * ME, (h % 2 + 1) * ME)
                pe.matmul(ps[:, 5, 0:P], qkv[r, U_MQ + h // 2, 0:P], qkv[r, U_MK + h // 2, 0:P], start=True, stop=True)
                pe.matmul(ps[:, 5, P:384], qkv[r, U_MQ + h // 2, P:SEQ], qkv[r, U_MK + h // 2, 0:SEQ],
                          start=True, stop=True).then_inc(score_done, 1)

            def turn_probs(h):
                pe.wait_ge(p_ready, 4 * (h + 1))
                for b in range(12):
                    ins = pe.transpose(ps[:, 2 + b // 4, (b % 4) * P:(b % 4 + 1) * P], logits[:, b * P:(b + 1) * P], ident)
                    if b % 4 == 3:
                        ins.then_inc(pt_done, 1)

            def values_prompt(h):
                pe.wait_ge(pt_evac, 3 * (h + 1))
                if h >= 1:
                    pe.wait_ge(o_evac, 2 * h)
                if h == 1:
                    pe.wait_ge(prod_done, 2 * NS)

                def run(out, steps):
                    for k, (lhsT, b) in enumerate(steps):
                        ins = pe.matmul(out, lhsT, probT[:, b * P:(b + 1) * P], start=k == 0, stop=k == len(steps) - 1)
                    return ins

                out = ps[h * DH:(h + 1) * DH, 6, :]
                v = [[vnat[:, t, g * P + h * DH:g * P + (h + 1) * DH] for t in range(2)] for g in range(NG)]
                run(out[:, 0:P], [(v[g][0], g) for g in range(NG)])
                run(out[:, P:256], [(v[g][t], 3 + 2 * g + t) for g in range(NG) for t in range(2)])
                out = ps[h % 2 * ME:(h % 2 + 1) * ME, 6, :]
                v = [vnat[:, t, 384 + h * ME:384 + (h + 1) * ME] for t in range(2)]
                run(out[:, 256:384], [(v[0], 9)])
                run(out[:, 384:512], [(v[t], 10 + t) for t in range(2)]).then_inc(o_done, 1)

            def branches(i):
                if i == 0:
                    pe.wait_ge(so_ready, 2)
                    pe.wait_ge(o_evac, 8)
                    pe.wait_ge(xc_ready, KC)
                    pe.wait_ge(cstd, 1)
                    pe.wait_ge(w_in[BR1 % 3], arrived[BR1])
                if i >= 2:
                    pe.wait_ge(br_read, i - 1)
                b0 = 3 * (i % 2)
                cols = slice(i * P, (i + 1) * P)
                pe.matmul(ps[:, b0 + 1, 0:T], rawb(BR1)[:, 0, cols], oT[:, 0], start=True, stop=True)
                for t in range(2):
                    pe.matmul(ps[:, b0 + 2, 0:T], rawb(BR1)[:, 1 + t, cols], oT[:, 1 + t], start=t == 0, stop=t == 1)
                if i == 0:
                    pe.wait_ge(cact_ready, 1)
                    pe.wait_ge(w_in[BR0 % 3], arrived[BR0])
                for t in range(KC):
                    ins = pe.matmul(ps[:, b0, 0:T], rawb(BR0)[:, t, cols], ca[:, t], start=t == 0, stop=t == KC - 1)
                ins.then_inc(br_done, 1)

            def project_out(i):
                pe.wait_ge(wlo_ready, NU + i + 1)
                if i >= 2:
                    pe.wait_ge(x1_ready, i - 1)
                for k in range(KD):
                    if i == 0:
                        pe.wait_ge(m_ready, k + 1)
                    ins = exact(ps[:, 6 + i % 2, 0:T], NU + i, k)
                ins.then_inc(wo_done, 1)

            def sum_x1():
                pe.wait_ge(x1_added, KD - 2)
                pe.matmul(ps[:, 0, 0:T], ones, rx[:, :], start=True, stop=False)
                pe.wait_ge(x1_squared, KD)
                pe.matmul(ps[:, 0, 0:T], ones, squ[:, (KD - 1) % 2], start=False, stop=True).then_inc(x1_summed, 1)

            turn_h()
            for j in range(NU):
                unit(j)
                if 1 <= j <= 4:
                    mean_square(j - 1)
                if 7 <= j <= 12:
                    mean_square(j - 3)
                if j == 5:
                    bias_tables()
                if 6 <= j <= 9:
                    turn_x(2 * j - 12)
                    turn_x(2 * j - 11)
                for i in NAT_AT.get(j, ()):
                    natural(i)
                for n in SPREAD_AT.get(j, ()):
                    spread_query(n)
                if j == CHAIN:
                    new_logits()
                if j == CHAIN + 1:
                    route()
                if j == CHAIN + 2:
                    turn_selection()
                if j == CHAIN + 3:
                    spread_selection()
                if j == CHAIN + 4:
                    turn_max()
                if j == CHAIN + 5:
                    spread_max()
                if j in TURN_AT:
                    turn_probs(TURN_AT.index(j))
                if j in VALUES_AT:
                    values_prompt(VALUES_AT.index(j))
                if j in SCORES_AT:
                    scores(SCORES_AT.index(j))
                if j == CHAIN + 7:
                    values_dilated()
                if j == CHAIN + 8:
                    denominators()
                    turn_dilated()
                    values_moba(0)
                if j == CHAIN + 9:
                    turn_moba(0)
                    values_moba(1)
            for n in range(2, NS):
                turn_moba(n - 1)
                values_moba(n)
                if n == 2:
                    turn_probs(2)
                    values_prompt(2)
                if n == 3:
                    scores(3)
                    conv_mean()
                if n == 5:
                    conv_var()
                    turn_probs(3)
                    values_prompt(3)
            turn_moba(NS - 1)
            for i in range(KD):
                branches(i)
            pe.sem_inc(ff_done, 4)
            for i in range(KD):
                project_out(i)
            sum_x1()

            def product(bank, s, rhs, first, last):
                for k in range(KD):
                    for a, b in ((0, 0), (0, 1), (1, 0)):
                        ins = pe.matmul(ps[:, bank, 0:T], ws[a][s][:, k], rhs[b][k],
                                        start=first and k == 0 and (a, b) == (0, 0),
                                        stop=last and k == KD - 1 and (a, b) == (1, 0))
                return ins

            pe.wait_ge(h_hi, KD)
            pe.wait_ge(h_lo, KD)
            with pe.Fori(0, 4) as i:
                for u in range(8):
                    pe.wait_ge(lo_ready, i * 8 + u + 1)
                    pe.wait_ge(bank_free, i * 8 + u + 1)
                    product(2 + u % 2, u % 4, [[hs[b][:, k] for k in range(KD)] for b in range(2)],
                            True, True).then_inc(ff_done, 1)

            def turn_output(i, m):
                pe.wait_ge(y_added, i * 2 + m + 3)
                for t, n in ((0, P), (1, P), (2, NS)):
                    ins = pe.transpose(ps[0:n, 6 + m, t * P:(t + 1) * P], yT[:, m, t * P:t * P + n], ident)
                ins.then_inc(y_turned, 1)

            def second(i, first):
                for u in range(8):
                    m = u // 4
                    pe.wait_ge(lo_ready, i * 8 + u + 33)
                    if u % 4 == 0:
                        pe.wait_ge(y_added, i * 2 + m + 1)
                    k0 = u % 4 * KD
                    if first and u < 4:
                        pe.wait_ge(a_ready, k0 + KD + 2)
                    product(4 + m, u % 4, [[as_[b][:, k0 + k] for k in range(KD)] for b in range(2)],
                            u % 4 == 0, u % 4 == 3).then_inc(ff_done, 1)
                    if u == 1 and not first:
                        turn_output(i - 1, 1)
                    if u == 5:
                        turn_output(i, 0)

            second(0, True)
            with pe.Fori(1, 4) as i:
                second(i, False)
            turn_output(3, 1)

        @block.scalar
        def _(sc):
            sc.dma_start(const[:, 0:NFIRST], A["const"][:, 0:NFIRST]).then_inc(first_in, 16)
            sc.dma_start(param[:, :], A["param"]).then_inc(small_in, 16)
            sc.wait_ge(first_in, 16)
            sc.activation(ssx[:, 6:7], cst("eps"), ACT.Sqrt)
            for k, t in enumerate((2, 0, 1)):
                n = NS if t == 2 else P
                sc.wait_ge(x_in[t], 16)
                sc.activation(xs[0:n, t], xnat[0:n, t], ACT.Square, accum_out=ssx[0:n, t:t + 1]).then_inc(x_squared, 1)
                sc.wait_ge(x_squared, k + 1)
                sc.activation(ssx[0:n, 3 + t:4 + t], ssx[0:n, t:t + 1], ACT.Sqrt, bias=cst("eps", n), scale=1.0 / D
                              ).then_inc(x_std, 1)
            sc.wait_ge(small_in, 16)

            def tables_out():
                sc.wait_ge(bias_made, 1)
                sc.copy(trow[:, :], ps[0:16, 2, 0:TW]).then_inc(rows_made, 1)
                sc.wait_ge(bias_made, 2)
                sc.copy(bias[:, :], ps[:, 3, 0:92]).then_inc(bias_copied, 2)

            def x_out(i):
                sc.wait_ge(x_turned, i + 1)
                sc.copy(xT[:, i], ps[:, 2 + i % 2, 0:T]).then_inc(x_copied, 1)

            def high(u):
                c = u // 3 if u < NU else WO0 + (u - NU) // 3
                if c == 0:
                    sc.wait_ge(unit_in[u], 16)
                else:
                    sc.wait_ge(w_in[c % 3], arrived[c])
                if WR <= u < NU + WR:
                    sc.wait_ge(z_done, u - WR + 1)
                elif u >= NU + WR:
                    sc.wait_ge(wo_done, u - NU - WR + 1)
                sc.copy(whi[u % WR][:, :, :], raw_unit(u)).then_inc(whi_ready, 1)

            for i in range(KD):
                sc.wait_ge(h_turned, i + 1)
                sc.activation(acts[0][:, i], ps[:, 4 + i % 4, 0:T], ACT.Copy, scale=par("g_mix", i)).then_inc(hin_hi, 1)
                if i == 2:
                    high(0)
            sc.dma_start(scv[:, :, :], A["state_conv"].rearrange("l n t c -> (l n t) c").rearrange(
                "(s q) c -> q s c", s=2)).then_inc(state_in, 16)
            for u in range(1, WR):
                high(u)

            def take(j):
                sc.wait_ge(z_done, j + 1)
                z = ps[:, j % 2, 0:T]
                if j in QK:
                    q = QK.index(j)
                    if q >= 2:
                        sc.wait_ge(ms_done, q - 1)
                if j in Q_UNITS:
                    zr = reversed_tiles(z[:, 0:SEQ])
                    sc.activation(squ[:, q % 2, 0:SEQ].rearrange("p (t c) -> p t c", c=P), zr, ACT.Square)
                    sc.activation(squ[:, q % 2, SEQ:T], z[:, SEQ:T], ACT.Square).then_inc(sq_ready, 1)
                    sc.copy(qkv[:, j, 0:SEQ].rearrange("p (t c) -> p t c", c=P), zr)
                    sc.copy(qkv[:, j, SEQ:T], z[:, SEQ:T]).then_inc(z_evac, 1)
                    return
                if j in QK:
                    sc.activation(squ[:, q % 2], z, ACT.Square).then_inc(sq_ready, 1)
                if j < 15:
                    sc.copy(qkv[:, j], z).then_inc(z_evac, 1)
                elif j < U_A:
                    sc.activation(cb[:, j - U_B], z, ACT.Sigmoid).then_inc(z_evac, 1)
                elif j < U_G:
                    sc.copy(ca[:, j - U_A], z).then_inc(z_evac, 1)
                else:
                    sc.activation(gates[:, j - U_G], z, ACT.Identity, bias=par("b_gate", j - U_G)).then_inc(z_evac, 1)

            def deviation(q):
                sc.wait_ge(ms_done, q + 1)
                if q >= 4:
                    sc.wait_ge(qn_done, q - 3)
                sc.activation(stdq[:, q % 4], ps[:, 6 + q % 2, 0:T], ACT.Sqrt, bias=cst("eps")).then_inc(std_done, 1)

            def natural_out(i):
                kind, u, col = NAT[i]
                bank = 2 + i % 2
                sc.wait_ge(nat_done, i + 1)
                if kind in "kv":
                    dst = knat if kind == "k" else vnat
                    sc.copy(dst[:, :, col:col + P], ps[:, bank, 0:256].rearrange("p (t c) -> p t c", t=2))
                if kind == "u":
                    sc.copy(unat[:, col:col + P], ps[0:HALO, bank, 0:P])
                if kind == "s":
                    sc.copy(usx[:, u, :, 0:HALO], ps[:, bank, 0:240].rearrange("p (n t) -> p n t", n=NS)
                            ).then_inc(nat_evac, 1)
                else:
                    rows, off = (qnat, col) if kind == "q" else (snat, {"k": 0, "v": 640, "u": 1280}[kind] + col)
                    sc.copy(rows[:, off:off + P], ps[0:NS, bank, 256:384]).then_inc(nat_evac, 1)

            def exps():
                sc.wait_ge(sub_ready, 4)
                sc.activation(sd, sd, ACT.Exp).then_inc(exp_done, 1)
                sc.activation(sm[:, :, :], sm[:, :, :], ACT.Exp).then_inc(exp_done, 1)
                sc.activation(ln[:, :], ln[:, :], ACT.Exp).then_inc(exp_done, 1)

            def values_out(n):
                if n == 0:
                    sc.wait_ge(pvd_done, 1)
                else:
                    sc.wait_ge(pvm_done, n)
                    sc.wait_ge(vt_done, n)
                if n == 1:
                    sc.copy(vd_t[:, :], ps[:, 7, 64:96])
                sc.copy(vo[:, :], ps[:, 7, 256:512]).then_inc(vo_ready, 1)

            def conv_square():
                sc.wait_ge(xc_ready, KC)
                sc.activation(csq[:, :, :], cb[:, :, :], ACT.Square).then_inc(csq_ready, 1)

            def conv_deviation():
                sc.wait_ge(var_done, 1)
                sc.activation(rx[:, :], ps[:, 1, 0:T], ACT.Sqrt, bias=cst("eps"), scale=1.0 / C).then_inc(cstd, 1)

            def conv_affine():
                sc.wait_ge(cy_ready, 1)
                for t in range(KC):
                    sc.activation(ca[:, t], cb[:, t], ACT.Identity, bias=par("ln_b", t), scale=par("ln_g", t)
                                  ).then_inc(cyn, 1)
                sc.wait_ge(cyn, KC)
                sc.activation(csq[:, :, :], ca[:, :, :], ACT.Sigmoid).then_inc(csg, 1)

            def prompt_exp(h):
                sc.wait_ge(l_ready, h + 1)
                for k, (lo, hi) in enumerate(((0, 384), (384, 1152), (1152, 1280), (1280, 1536))):
                    sc.activation(logits[:, lo:hi], logits[:, lo:hi], ACT.Exp, bias=nmax[:, k:k + 1],
                                  accum_out=psum_[:, k:k + 1]).then_inc(p_exp, 1)

            def prompt_scale(h):
                sc.wait_ge(inv_ready, h + 1)
                for k, (lo, hi) in enumerate(((0, 384), (384, 1152), (1152, 1280), (1280, 1536))):
                    sc.activation(logits[:, lo:hi], logits[:, lo:hi], ACT.Copy, scale=pinv[:, k:k + 1]
                                  ).then_inc(p_ready, 1)

            def probs_out(h):
                if h == 0:
                    sc.wait_ge(conv_stored, 16 * 3)
                for b in range(3):
                    sc.wait_ge(pt_done, 3 * h + b + 1)
                    if h >= 1 and b == 0:
                        sc.wait_ge(o_done, h)
                    sc.copy(probT[:, b * 512:(b + 1) * 512], ps[:, 2 + b, :]).then_inc(pt_evac, 1)

            def outputs_out(h):
                sc.wait_ge(o_done, h + 1)
                r = slice(h * DH, (h + 1) * DH)
                sc.copy(oT[r, 0, 0:SEQ].rearrange("p (t c) -> p t c", c=P), reversed_tiles(ps[r, 6, 0:256])).then_inc(o_evac, 1)
                r = slice(h % 2 * ME, (h % 2 + 1) * ME)
                sc.copy(oT[r, 1 + h // 2, 0:SEQ].rearrange("p (t c) -> p t c", c=P), reversed_tiles(ps[r, 6, 256:512])).then_inc(o_evac, 1)

            for j in range(NU):
                take(j)
                if j + WR < NU:
                    high(j + WR)
                if 1 <= j <= 4:
                    deviation(j - 1)
                if 7 <= j <= 12:
                    deviation(j - 3)
                if j == 5:
                    tables_out()
                if 6 <= j <= 9:
                    x_out(2 * j - 12)
                    x_out(2 * j - 11)
                for i in NAT_AT.get(j, ()):
                    natural_out(i)
                if j - 1 in SCORES_AT[:2]:
                    prompt_exp(SCORES_AT.index(j - 1))
                if j == CHAIN + 6:
                    exps()
                if j + 1 in TURN_AT:
                    prompt_scale(TURN_AT.index(j + 1))
                if j in TURN_AT:
                    probs_out(TURN_AT.index(j))
                if j in VALUES_AT:
                    outputs_out(VALUES_AT.index(j))
                if CHAIN + 7 <= j <= CHAIN + 9:
                    values_out(j - CHAIN - 7)
                if j == NU - 2:
                    prompt_exp(2)
            prompt_scale(2)
            values_out(3)
            probs_out(2)
            outputs_out(2)
            values_out(4)
            values_out(5)
            prompt_exp(3)
            conv_square()
            values_out(6)
            prompt_scale(3)
            conv_deviation()
            probs_out(3)
            outputs_out(3)
            conv_affine()
            values_out(7)
            values_out(8)

            def high_merged(i):
                sc.wait_ge(m_sum, i + 1)
                sc.copy(acts[0][:, i], mtmp[:, i % 2, 0]).then_inc(m_hi, 1)

            gv = gates[:, :, :].rearrange("p (b i) t -> p b i t", b=3)
            for i in range(KD):
                sc.activation(gv[:, :, i], gv[:, :, i], ACT.Sigmoid).then_inc(gate_ready, 1)
                if 1 <= i <= WR:
                    high(NU + i - 1)
                if i >= 2:
                    high_merged(i - 2)
            high_merged(KD - 2)
            high_merged(KD - 1)

            def high_ff1(i, u):
                s, n = (u // 2) % 4, u // 8
                sc.wait_ge(fw_in[s], i * 16 + 16 * (n + 1))
                sc.wait_ge(ff_done, i * 8 + u + 1)
                sc.copy(ws[0][u % 4][:, :, :], weights1(s, u % 2)).then_inc(hi_ready, 1)

            def high_ff2(i, u):
                s, n = (u // 2) % 4, u // 8
                sc.wait_ge(fw_in[s], i * 16 + 16 * (n + 5))
                sc.wait_ge(ff_done, i * 8 + u + 33)
                sc.copy(ws[0][u % 4][:, :, :], weights2(s, u % 2)).then_inc(hi_ready, 1)

            sc.wait_ge(m_ready, KD)
            for i in range(KD):
                sc.wait_ge(x1_ready, i + 1)
                sc.activation(hs[0][:, i], xT[:, i], ACT.Copy, scale=par("g_ffn", i)).then_inc(h_hi, 1)
                if i == 0:
                    sc.activation(rx[:, :], xT[:, 0], ACT.Square).then_inc(x1_squared, 1)
                else:
                    if i >= 3:
                        sc.wait_ge(x1_added, i - 2)
                    sc.activation(squ[:, i % 2], xT[:, i], ACT.Square).then_inc(x1_squared, 1)
                if i < KD - WR:
                    high(NU + i + WR)
                if 5 <= i < 7:
                    high_ff1(0, i - 5)
            high_ff1(0, 2)
            sc.wait_ge(x1_summed, 1)
            sc.activation(rx[:, :], ps[:, 0, 0:T], ACT.Sqrt, bias=cst("eps"), scale=1.0 / D).then_inc(x1_std, 1)

            def hidden(i, u):
                sc.wait_ge(bank_free, i * 8 + u + 3)
                sc.wait_ge(a_ready, i * 8 + u + 1)
                sc.activation(ra[:, u % 2], rl[:, u % 2], ACT.Square).then_inc(ra_ready, 1)

            with sc.Fori(0, 3) as i:
                for u in range(8):
                    high_ff1(i, u + 3)
                    hidden(i, u)
            for u in range(8):
                if u < 5:
                    high_ff1(3, u + 3)
                else:
                    high_ff2(0, u - 5)
                hidden(3, u)

            def rows_back(i, m):
                sc.wait_ge(y_turned, i * 2 + m + 1)
                sc.copy(ynat[:, bass.ds(i * 6 + m * 3, 2), :], ps[:, 6 + m, 0:256].rearrange("p (t c) -> p t c", t=2))
                sc.copy(ynat[0:NS, bass.ds(i * 6 + m * 3 + 2, 1), :], ps[0:NS, 6 + m:7 + m, 256:384]).then_inc(y_evac, 1)

            for u in range(8):
                high_ff2(0, u + 3)
            rows_back(0, 0)
            with sc.Fori(1, 3) as i:
                for u in range(8):
                    high_ff2(i, u + 3)
                    if u == 2:
                        rows_back(i - 1, 1)
                rows_back(i, 0)
            for u in range(5):
                high_ff2(3, u + 3)
                if u == 2:
                    rows_back(2, 1)
            rows_back(3, 0)
            rows_back(3, 1)

        @block.vector
        def _(v):
            steps = [0]

            def step(ins):
                steps[0] += 1
                ins.then_inc(dve, 1)
                v.wait_ge(dve, steps[0])

            v.wait_ge(page_in, 16)
            v.wait_ge(first_in, 16)
            v.tensor_scalar(pidx[:, :], ptab[:, :], float(PAGE // ROWS), cst("sub8"), ALU.mult, ALU.add
                            ).then_inc(idx_ready, 1)
            for k, t in enumerate((2, 0, 1)):
                n = NS if t == 2 else P
                v.wait_ge(x_std, k + 1)
                step(v.reciprocal(ssx[0:n, t:t + 1], ssx[0:n, 3 + t:4 + t]))
                v.tensor_scalar(xs[0:n, t], xnat[0:n, t], ssx[0:n, t:t + 1], None, ALU.mult).then_inc(x_scaled, 1)
            v.wait_ge(small_in, 16)
            for i in range(KD):
                v.wait_ge(h_turned, i + 1)
                v.wait_ge(hin_hi, i + 1)
                v.scalar_tensor_tensor(acts[1][:, i], ps[:, 4 + i % 4, 0:T], par("g_mix", i), acts[0][:, i].bitcast(F32),
                                       ALU.mult, ALU.subtract).then_inc(h_ready, 1)
            v.wait_ge(const_in, 16)

            def norm_heads(q):
                u = QK[q]
                g = par("mqn" if q < 2 else "mkn" if q < 4 else "dqn" if q < 7 else "dkn")
                v.wait_ge(std_done, q + 1)
                v.wait_ge(z_evac, u + 1)
                step(v.reciprocal(stdq[:, q % 4], stdq[:, q % 4]))
                v.scalar_tensor_tensor(qkv[:, u], qkv[:, u], g, stdq[:, q % 4], ALU.mult, ALU.mult).then_inc(qn_done, 1)

            def score_cache(n):
                k = kv[n % 2][:, :].rearrange("p (r c) -> p r c", c=MW)
                v.wait_ge(kv_in[n % 2], kv_arrived[n])
                v.wait_ge(qb_done, n + 1)
                q = ps[:, SPREAD_BANK[n]:SPREAD_BANK[n] + 1, 0:MW].broadcast_to([P, ROWS, MW])
                v.tensor_tensor(k, k, q, ALU.mult).then_inc(prod_done, 1)

            def sum_heads(n):
                v.wait_ge(prod_done, n + 1)
                v.tensor_reduce(sm[:, n], kv[n % 2][:, :].rearrange("p (a e) -> p a e", e=ME), AX.X, ALU.add
                                ).then_inc(kred_done, 1)

            def score_state():
                v.wait_ge(kv_in[IT_SK % 2], kv_arrived[IT_SK])
                for n in range(NS):
                    v.wait_ge(qb_done, NS + n + 1)
                    v.tensor_tensor(stk[:, :, n], stk[:, :, n],
                                    ps[:, SPREAD_BANK[NS + n], 0:384].rearrange("p (g c) -> p g c", g=NG), ALU.mult
                                    ).then_inc(prod_done, 1)
                v.wait_ge(prod_done, 2 * NS)
                v.tensor_reduce(sd, stk[:, :, :, :].rearrange("p g n (h e) -> p (g n h) e", e=DH), AX.X, ALU.add
                                ).then_inc(kred_done, 1)

            def gate_conv():
                v.wait_ge(z_evac, U_G)
                v.tensor_tensor(uext[:, :, HALO:], ca[:, :, 0:SEQ], cb[:, :, 0:SEQ], ALU.mult).then_inc(u_ready, 1)
                v.tensor_tensor(usx[:, :, :, HALO], ca[:, :, SEQ:T], cb[:, :, SEQ:T], ALU.mult).then_inc(u_ready, 1)

            def taps(lo, hi):
                w = param[:, POFF["conv_w"][0]:POFF["conv_w"][1]].rearrange("p (c k) -> p c k", c=KC)
                for k in range(lo, hi):
                    for c in range(KC):
                        src, acc = uext[:, c, k:k + SEQ], ca[:, c, 0:SEQ]
                        if k == 0:
                            v.wait_ge(u_ready, 2)
                            v.wait_ge(padded, 1)
                            v.tensor_scalar(acc, src, w[:, c, 0:1], par("conv_b", c), ALU.mult, ALU.add
                                            ).then_inc(conv_step, 1)
                        else:
                            v.wait_ge(conv_step, KC * (k - 1) + c + 1)
                            v.scalar_tensor_tensor(acc, src, w[:, c, k:k + 1], acc, ALU.mult, ALU.add
                                                   ).then_inc(conv_step, 1)

            def sample_taps():
                v.wait_ge(nat_evac, N_U)
                v.wait_ge(u_ready, 2)
                w = param[:, POFF["conv_w"][0]:POFF["conv_w"][1]].rearrange("p (c k) -> p c k", c=KC)
                for c in range(KC):
                    step(v.tensor_tensor(usx[:, c], usx[:, c], w[:, c:c + 1, :].broadcast_to([P, NS, TAPS]), ALU.mult))
                step(v.tensor_reduce(ca[:, :, SEQ:T], usx[:, :, :, :], AX.X, ALU.add))
                b = param[:, POFF["conv_b"][0]:POFF["conv_b"][1]].unsqueeze(2).broadcast_to([P, KC, NS])
                v.wait_ge(conv_step, KC * TAPS)
                v.tensor_tensor(ca[:, :, SEQ:T], ca[:, :, SEQ:T], b, ALU.add).then_inc(conv_done, 1)

            def nh(ap):
                return ap.rearrange("p (n h) -> p n h", h=4)

            def new_products():
                v.wait_ge(z_evac, U_B)
                v.wait_ge(qn_done, len(QK))
                step(v.tensor_tensor(pnd[:, :, :], qkv[:, U_DQ:U_DQ + 3, SEQ:T], qkv[:, U_DK:U_DK + 3, SEQ:T], ALU.mult))
                step(v.tensor_tensor(pnm[:, :, :], qkv[:, U_MQ:U_MQ + 2, SEQ:T], qkv[:, U_MK:U_MK + 2, SEQ:T], ALU.mult))
                a = pnd[:, :, :].rearrange("p g n -> p (g n)").unsqueeze(2).broadcast_to([P, NG * NS, HPG])
                b = cst("hmask").unsqueeze(1).broadcast_to([P, NG * NS, HPG])
                v.tensor_tensor(rnd[:, :, :], a, b, ALU.mult).then_inc(new_ready, 1)
                a = pnm[:, :, :].unsqueeze(3).broadcast_to([P, 2, NS, MH])
                b = cst("mmask").rearrange("p (t h) -> p t h", t=2).unsqueeze(2).broadcast_to([P, 2, NS, MH])
                v.tensor_tensor(rnm[:, :, :, :], a, b, ALU.mult).then_inc(new_ready, 1)

            def rows_n(lo, width):
                return bias[:, lo:lo + width].unsqueeze(1).broadcast_to([P, NS, width])

            def sample_logits():
                v.wait_ge(new_dot, 1)
                v.wait_ge(bias_copied, 2)
                for g in range(4):
                    cols = slice(g * 32, g * 32 + 32)
                    v.scalar_tensor_tensor(nh(ln[:, cols]), nh(ps[:, 7, cols]), s_d if g < NG else s_m,
                                           rows_n(76 + 4 * g, 4), ALU.mult, ALU.add).then_inc(new_read, 1)
                v.wait_ge(kred_done, NS + 1)
                v.tensor_reduce(rt[:, :].rearrange("p (n h) -> p n h", h=MH),
                                sm[:, :, :].rearrange("p n (r h) -> p n h r", h=MH), AX.X, ALU.add).then_inc(route_ready, 1)
                for g in range(NG):
                    cols = slice(g * 32, g * 32 + 32)
                    ins = v.scalar_tensor_tensor(nh(sd[:, cols]), nh(sd[:, cols]), s_d, rows_n(64 + 4 * g, 4),
                                                 ALU.mult, ALU.add)
                step(ins)
                step(v.scalar_tensor_tensor(sm[:, :, :], sm[:, :, :], s_m, rows_n(0, 64), ALU.mult, ALU.add))

            def select_blocks():
                v.wait_ge(route_dot, 1)
                step(v.tensor_copy(r32[:, :], ps[0:32, 7, 128:136]))
                step(v.max(top[:, :], r32[:, :]))
                step(v.max_index(topi[:, :], top[:, :], r32[:, :]))
                step(v.tensor_copy(topf[:, :], topi[:, :]))
                io = cst("iota", 32)
                step(v.tensor_scalar(selb[:, :], io, topf[:, 0:1], None, ALU.is_equal))
                for k in range(1, TOPK):
                    step(v.scalar_tensor_tensor(selb[:, :], io, topf[:, k:k + 1], selb[:, :], ALU.is_equal, ALU.add))
                v.tensor_scalar(selb[:, :], selb[:, :], -NEG, NEG, ALU.mult, ALU.add).then_inc(sel_ready, 1)

            def selection_row():
                v.wait_ge(sel_turned, 1)
                v.tensor_copy(selT[:, :], ps[0:NB, 7, 136:168]).then_inc(selT_ready, 1)

            def sample_maxima():
                v.wait_ge(sel_spread, 1)
                mask = nh(ps[:, 7, 168:200]).unsqueeze(2).broadcast_to([P, NS, ROWS, MH])
                m4 = sm[:, :, :].rearrange("p n (r h) -> p n r h", h=MH)
                v.tensor_tensor(m4, m4, mask, ALU.add).then_inc(sel_read, 1)
                v.wait_ge(sel_read, 1)
                v.tensor_reduce(mc[:, 0:32], sd.rearrange("p (g m) -> p m g", g=NG), AX.X, ALU.max
                                ).then_inc(mc_ready, 1)
                v.tensor_reduce(nh(mc[:, 32:64]), sm[:, :, :].rearrange("p n (r h) -> p n h r", h=MH), AX.X, ALU.max
                                ).then_inc(mc_ready, 1)
                step(v.tensor_reduce(lmax[:, :], ln[:, 0:96].rearrange("p (g m) -> p m g", g=NG), AX.X, ALU.max))

            def spread_maxima():
                v.wait_ge(mc_turned, 1)
                step(v.tensor_reduce(mm[:, :], ps[0:64, 7, 200:328], AX.X, ALU.max))
                v.tensor_scalar(dg[:, :], ident[0:64, 0:64], mm[:, :], None, ALU.mult).then_inc(dg_ready, 1)

            def subtract_maxima():
                v.wait_ge(max_spread, 1)
                step(v.tensor_tensor(gmx[:, 0:32], ps[:, 7, 328:360], lmax[:, :], ALU.max))
                step(v.tensor_tensor(gmx[:, 32:64], ps[:, 7, 360:392], ln[:, 96:128], ALU.max))
                gd = gmx[:, 0:32].unsqueeze(1).broadcast_to([P, NG, 32])
                v3 = sd.rearrange("p (g m) -> p g m", g=NG)
                v.tensor_tensor(v3, v3, gd, ALU.subtract).then_inc(sub_ready, 1)
                m4 = sm[:, :, :].rearrange("p n (r h) -> p n r h", h=MH)
                gm = nh(gmx[:, 32:64]).unsqueeze(2).broadcast_to([P, NS, ROWS, MH])
                v.tensor_tensor(m4, m4, gm, ALU.subtract).then_inc(sub_ready, 1)
                v3 = ln[:, 0:96].rearrange("p (g m) -> p g m", g=NG)
                v.tensor_tensor(v3, v3, gd, ALU.subtract).then_inc(sub_ready, 1)
                v.tensor_tensor(ln[:, 96:128], ln[:, 96:128], gmx[:, 32:64], ALU.subtract).then_inc(sub_ready, 1)

            def sample_sums():
                v.wait_ge(exp_done, 3)
                v.tensor_reduce(ssum[:, 0:32], sd.rearrange("p (g m) -> p m g", g=NG), AX.X, ALU.add
                                ).then_inc(sum_ready, 1)
                v.tensor_reduce(nh(ssum[:, 32:64]), sm[:, :, :].rearrange("p n (r h) -> p n h r", h=MH), AX.X, ALU.add
                                ).then_inc(sum_ready, 1)
                step(v.tensor_reduce(lmax[:, :], ln[:, 0:96].rearrange("p (g m) -> p m g", g=NG), AX.X, ALU.add))

            def sample_denominators():
                v.wait_ge(den_dot, 1)
                v.tensor_tensor(gmx[:, 0:32], ps[:, 7, 128:160], lmax[:, :], ALU.add)
                v.tensor_tensor(gmx[:, 32:64], ps[:, 7, 160:192], ln[:, 96:128], ALU.add).then_inc(den_read, 1)
                v.wait_ge(den_read, 1)
                step(v.reciprocal(rden[:, :], gmx[:, :]))

            def outputs_dilated():
                v.wait_ge(vo_ready, 2)
                vd = qkv[:, U_DV:U_DV + 3, SEQ:T].unsqueeze(3).broadcast_to([P, NG, NS, HPG])
                t1v = t1[:, :, :].rearrange("p g (n h) -> p g n h", h=HPG)
                step(v.tensor_tensor(t1v, ln[:, 0:96].rearrange("p (g n h) -> p g n h", g=NG, h=HPG), vd, ALU.mult))
                step(v.tensor_reduce(lmax[:, :], t1[:, :, :].rearrange("p g m -> p m g"), AX.X, ALU.add))
                step(v.tensor_tensor(lmax[:, :], lmax[:, :], vd_t[:, :], ALU.add))
                step(v.tensor_tensor(lmax[:, :], lmax[:, :], rden[:, 0:32], ALU.mult))
                step(v.tensor_tensor(nh(lmax[:, :]), nh(lmax[:, :]), cst("hmask").unsqueeze(1).broadcast_to([P, NS, HPG]),
                                     ALU.mult))
                v.tensor_reduce(oT[:, 0, SEQ:T], nh(lmax[:, :]), AX.X, ALU.add).then_inc(so_ready, 1)

            def outputs_moba():
                v.wait_ge(vt_done, NS + 1)
                vm = qkv[:, U_MV:U_MV + 2, SEQ:T].unsqueeze(3).broadcast_to([P, 2, NS, MH])
                t2v = t2[:, :, :].rearrange("p t (n h) -> p t n h", h=MH)
                pn = nh(ln[:, 96:128]).unsqueeze(1).broadcast_to([P, 2, NS, MH])
                step(v.tensor_tensor(t2v, pn, vm, ALU.mult))
                step(v.tensor_tensor(t2[:, :, :], t2[:, :, :], ps[:, 7, 0:64].rearrange("p (t m) -> p t m", t=2), ALU.add))
                step(v.tensor_tensor(t2[:, :, :], t2[:, :, :], rden[:, 32:64].unsqueeze(1).broadcast_to([P, 2, 32]), ALU.mult))
                mask = cst("mmask").rearrange("p (t h) -> p t h", t=2).unsqueeze(2).broadcast_to([P, 2, NS, MH])
                step(v.tensor_tensor(t2v, t2v, mask, ALU.mult))
                v.tensor_reduce(oT[:, 1:3, SEQ:T], t2v, AX.X, ALU.add).then_inc(so_ready, 1)

            def conv_center():
                v.wait_ge(mean_done, 1)
                for t in range(KC):
                    v.scalar_tensor_tensor(cb[:, t], ps[:, 0, 0:T], -1.0 / C, ca[:, t], ALU.mult, ALU.add
                                           ).then_inc(xc_ready, 1)

            def conv_scale():
                v.wait_ge(cstd, 1)
                step(v.reciprocal(rx[:, :], rx[:, :]))
                v.tensor_tensor(cb[:, :, :], cb[:, :, :], rx[:, :].unsqueeze(1).broadcast_to([P, KC, T]), ALU.mult
                                ).then_inc(cy_ready, 1)

            def conv_swish():
                v.wait_ge(csg, 1)
                v.tensor_tensor(ca[:, :, :], ca[:, :, :], csq[:, :, :], ALU.mult).then_inc(cact_ready, 1)

            def prompt_logits(h):
                v.wait_ge(score_done, h + 1)
                v.wait_ge(e_in[h % 2], 16 * (h // 2 + 1))
                if h == 0:
                    v.wait_ge(stored, 16 * 16)
                else:
                    v.wait_ge(pt_done, 3 * h)
                e = ebias[:, h % 2]
                v.scalar_tensor_tensor(logits[:, 0:384].rearrange("p (g c) -> p g c", g=NG),
                                       ps[:, 2, 0:384].rearrange("p (g c) -> p g c", g=NG), s_d, e[:, 0:3, P:256],
                                       ALU.mult, ALU.add)
                v.scalar_tensor_tensor(logits[:, 384:1152].rearrange("p (g c) -> p g c", g=NG),
                                       ps_s1[:, 0:768].rearrange("p (g c) -> p g c", g=NG), s_d, e[:, 0:3, :],
                                       ALU.mult, ALU.add)
                v.scalar_tensor_tensor(logits[:, 1152:1280], ps[:, 5, 0:P], s_m, e[:, 3, P:256], ALU.mult, ALU.add)
                step(v.scalar_tensor_tensor(logits[:, 1280:1536], ps[:, 5, P:384], s_m, e[:, 3, :], ALU.mult, ALU.add))
                for k, (lo, hi) in enumerate(((0, 384), (384, 1152), (1152, 1280), (1280, 1536))):
                    ins = v.tensor_reduce(nmax[:, k:k + 1], logits[:, lo:hi], AX.X, ALU.max, negate=True)
                ins.then_inc(l_ready, 1)

            def prompt_probs(h):
                v.wait_ge(p_exp, 4 * (h + 1))
                if h:
                    v.wait_ge(p_ready, 4 * h)
                v.reciprocal(pinv[:, :], psum_[:, :]).then_inc(inv_ready, 1)

            norm_heads(0)
            norm_heads(1)
            for n, qs in enumerate(((2, 3), (4, 5, 6), (7, 8, 9), ())):
                score_cache(n)
                sum_heads(n)
                for q in qs:
                    norm_heads(q)
            score_cache(4)
            gate_conv()
            sum_heads(4)
            score_cache(5)
            taps(0, 13)
            prompt_logits(0)
            sum_heads(5)
            new_products()
            score_cache(6)
            prompt_probs(0)
            sum_heads(6)
            score_cache(7)
            prompt_logits(1)
            sum_heads(7)
            prompt_probs(1)
            score_state()
            sample_logits()
            select_blocks()
            selection_row()
            sample_maxima()
            spread_maxima()
            subtract_maxima()
            taps(13, 19)
            sample_sums()
            taps(19, 21)
            sample_denominators()
            prompt_logits(2)
            taps(21, 27)
            prompt_probs(2)
            taps(27, TAPS)
            sample_taps()
            prompt_logits(3)
            conv_center()
            outputs_dilated()
            prompt_probs(3)
            conv_scale()
            conv_swish()
            outputs_moba()

            def merge(i):
                v.wait_ge(br_done, i + 1)
                v.wait_ge(gate_ready, i + 1)
                if i >= 2:
                    v.wait_ge(m_ready, i - 1)
                b0 = 3 * (i % 2)
                g = gates[:, :, :].rearrange("p (b i) t -> p b i t", b=3)[:, :, i]
                mt = mtmp[:, i % 2]
                v.tensor_tensor(mt, ps[:, b0:b0 + 3, 0:T], g, ALU.mult).then_inc(br_read, 1)
                v.wait_ge(br_read, i + 1)
                step(v.tensor_tensor(mt[:, 0], mt[:, 0], mt[:, 1], ALU.add))
                v.tensor_tensor(mt[:, 0], mt[:, 0], mt[:, 2], ALU.add).then_inc(m_sum, 1)

            def low_merged(i):
                v.wait_ge(m_hi, i + 1)
                v.tensor_tensor(acts[1][:, i], mtmp[:, i % 2, 0], acts[0][:, i].bitcast(F32), ALU.subtract
                                ).then_inc(m_ready, 1)

            for i in range(KD):
                merge(i)
                if i:
                    low_merged(i - 1)
            low_merged(KD - 1)

            def low_x1(k):
                v.wait_ge(h_hi, k + 1)
                v.scalar_tensor_tensor(hs[1][:, k], xT[:, k], par("g_ffn", k), hs[0][:, k].bitcast(F32),
                                       ALU.mult, ALU.subtract).then_inc(h_lo, 1)

            def low(i, u, second):
                v.wait_ge(hi_ready, i * 8 + u + 1 + (32 if second else 0))
                s = (u // 2) % 4
                v.tensor_tensor(ws[1][u % 4][:, :, :], (weights2 if second else weights1)(s, u % 2),
                                ws[0][u % 4][:, :, :].bitcast(F32), ALU.subtract).then_inc(lo_ready, 1)

            for i in range(KD):
                v.wait_ge(wo_done, i + 1)
                v.tensor_tensor(xT[:, i], xT[:, i], ps[:, 6 + i % 2, 0:T], ALU.add).then_inc(x1_ready, 1)
                if i:
                    low_x1(i - 1)
                if i >= 2:
                    v.wait_ge(x1_squared, i)
                    if i >= 3:
                        v.wait_ge(x1_added, i - 2)
                    v.tensor_tensor(rx[:, :], rx[:, :], squ[:, (i - 1) % 2], ALU.add).then_inc(x1_added, 1)
                if i == 6:
                    low(0, 0, False)
            low_x1(KD - 1)
            low(0, 1, False)
            v.sem_inc(a_ready, 2)
            v.sem_inc(y_added, 2)
            v.sem_inc(bank_free, 2)
            v.wait_ge(x1_std, 1)
            step(v.reciprocal(rinv[:, :], rx[:, :]))
            low(0, 2, False)

            def hidden_split(i, u, ahead):
                v.wait_ge(ff_done, i * 8 + u + 5)
                v.scalar_tensor_tensor(rl[:, u % 2], ps[:, 2 + u % 2, 0:T], 0.0, rinv[:, :], ALU.max, ALU.mult
                                       ).then_inc(bank_free, 1)
                low(*ahead)
                v.wait_ge(ra_ready, i * 8 + u + 1)
                t = i * 8 + u
                v.tensor_copy(as_[0][:, bass.ds(t, 1)], ra[:, u % 2:u % 2 + 1]).then_inc(ahi_ready, 1)
                v.wait_ge(ahi_ready, i * 8 + u + 1)
                v.tensor_tensor(as_[1][:, bass.ds(t, 1)], ra[:, u % 2:u % 2 + 1], as_[0][:, bass.ds(t, 1)].bitcast(F32),
                                ALU.subtract).then_inc(a_ready, 1)

            with v.Fori(0, 3) as i:
                for u in range(8):
                    hidden_split(i, u, (i, u + 3, False))
            for u in range(5):
                hidden_split(3, u, (3, u + 3, False))
            for u in range(5, 8):
                hidden_split(3, u, (0, u - 5, True))

            def add_residual(i, m):
                v.wait_ge(ff_done, i * 8 + 4 * m + 40)
                v.tensor_tensor(yT[:, m:m + 1], xT[:, bass.ds(i * 2 + m, 1)], ps[:, 4 + m:5 + m, 0:T], ALU.add
                                ).then_inc(y_added, 1)

            with v.Fori(0, 3) as i:
                for u in range(8):
                    low(i, u + 3, True)
                    if u in (3, 7):
                        add_residual(i, u // 4)
            for u in range(5):
                low(3, u + 3, True)
                if u == 3:
                    add_residual(3, 0)
            add_residual(3, 1)



_PLAIN = ['x_prompt', 'x_sample', 'state_conv', 'state_dil_k0', 'state_dil_v0', 'state_dil_k1', 'state_dil_v1',
          'state_dil_k2', 'state_dil_v2', 'cache_k', 'cache_v', 'rel_bias', 'w_in', 'w_conv_out', 'w_dil_out',
          'w_moba_out', 'w_out', 'w_ff1', 'w_ff2']
_OUTS = [("y_prompt", (1, SEQ, D)), ("y_sample", (NS, 1, D)), ("conv_p", (1, 1, HALO, C)), ("conv_s", (1, NS, HALO, C))] \
    + [(f"d{x}{g}_p", (1, 1, min(GROUPS[g][0], SEQ), HPG, DH)) for g in range(NG) for x in "kv"] \
    + [(f"d{x}{g}_s", (1, NS, GROUPS[g][0], HPG, DH)) for g in range(NG) for x in "kv"] \
    + [("k_p", (1, 1, SEQ, MH, ME)), ("v_p", (1, 1, SEQ, MH, ME)), ("k_s", (1, NS, 1, MH, ME)), ("v_s", (1, NS, 1, MH, ME))]


def kernel(**inputs):
    import concourse.bacc as _bacc
    from concourse.bass_utils import run_bass_kernel_spmd as _run

    def cols(a, k):
        return np.ascontiguousarray(np.asarray(a).reshape(k, P).T)

    a = {n: np.ascontiguousarray(inputs[n]) for n in _PLAIN}
    a["const"], a["hot"], a["group"] = shape_constants()
    a["param"] = np.concatenate(
        [cols(inputs["norm_mix_g"], KD), cols(inputs["norm_ffn_g"], KD), cols(inputs["b_gate"], 3 * KD),
         np.asarray(inputs["conv_w"])[0].reshape(TAPS, KC, P).transpose(2, 1, 0).reshape(P, KC * TAPS),
         cols(inputs["conv_b"], KC), cols(inputs["conv_ln_g"], KC), cols(inputs["conv_ln_b"], KC)]
        + [np.tile(np.asarray(inputs[n])[0], r)[:, None] for n, r in
           (("dil_qn_g", 4), ("dil_kn_g", 4), ("moba_qn_g", 2), ("moba_kn_g", 2))], axis=1)
    a["page_rows"] = np.ascontiguousarray(np.repeat(np.asarray(inputs["page_table"]).T, PAGE // ROWS, axis=0))

    nc = _bacc.Bacc("TRN2", target_bir_lowering=False, num_devices=1)
    arrays, A, O = {}, {}, {}
    for n, x in a.items():
        arrays[f"in_{n}"] = x
        A[n] = nc.dram_tensor(f"in_{n}", x.shape, mybir.dt.from_np(x.dtype), kind="ExternalInput").ap()
    for n, s in _OUTS:
        O[n] = nc.dram_tensor(f"out_{n}", s, F32, kind="ExternalOutput").ap()
    build_layer(nc, A, O)
    r = _run(nc, [arrays], core_ids=[0])
    return tuple(r.results[0][f"out_{n}"] for n, _ in _OUTS)
```
